# Optimizing a Trainium2 kernel written in Bass

```python
import math, functools
import jax, jax.numpy as jnp
from jax import lax
import numpy as np

D_MODEL = 1024
BATCH = 1
SEQ = 512
DEPTH = 1
DEC_BATCH = 1
DEC_SEQ = 64
PAST_LEN = 256

CHUNK = 64
QBLOCK = 128
HEAD_DIM = 64
A_HEADS = 8
A_KV_HEADS = 2
IDX_HEADS = 8
IDX_DIM = 64
B_HEADS = 4
TOPK_MAX = 256
D_FF = -(-8 * D_MODEL // (3 * 256)) * 256
ROPE_THETA = 10000.0
EPS = 1e-6
A_WIDTH = A_HEADS * HEAD_DIM
A_KV_WIDTH = A_KV_HEADS * HEAD_DIM
IDX_Q_WIDTH = IDX_HEADS * IDX_DIM
B_QK_WIDTH = B_HEADS * 2 * HEAD_DIM
B_V_WIDTH = B_HEADS * 2 * HEAD_DIM
IN_SPLITS = (A_WIDTH, A_KV_WIDTH, A_KV_WIDTH, IDX_Q_WIDTH, IDX_DIM, IDX_HEADS,
             B_QK_WIDTH, B_QK_WIDTH, B_V_WIDTH, D_MODEL, D_MODEL)
IN_COLS = sum(IN_SPLITS)
SPLIT_POINTS = tuple(sum(IN_SPLITS[:i + 1]) for i in range(len(IN_SPLITS) - 1))
IDX_SCALE = (IDX_HEADS * IDX_DIM) ** -0.5
ATTN_SCALE = HEAD_DIM ** -0.5

kernel_name = 'hybrid_dsa_diff_stream_encoder_step'

def rms_norm(x, g):
    xf = x.astype(jnp.float32)
    y = xf * lax.rsqrt(jnp.mean(xf * xf, axis=-1, keepdims=True) + EPS)
    return (y * g).astype(x.dtype)

def modulate(h, shift, scale):
    return h * (1 + scale[:, None]) + shift[:, None]

def rope(x, pos):
    half = x.shape[-1] // 2
    inv = 1.0 / (ROPE_THETA ** (jnp.arange(half, dtype=jnp.float32) / half))
    ang = pos.astype(jnp.float32)[:, None] * inv[None, :]
    shp = (ang.shape[0],) + (1,) * (x.ndim - 3) + (half,)
    cos = jnp.cos(ang).reshape(shp)
    sin = jnp.sin(ang).reshape(shp)
    x1 = x[..., :half].astype(jnp.float32)
    x2 = x[..., half:].astype(jnp.float32)
    out = jnp.concatenate([x1 * cos - x2 * sin, x2 * cos + x1 * sin], axis=-1)
    return out.astype(x.dtype)

def project(h, pos, w_in):
    bn, s, _ = h.shape
    z = h @ w_in
    qa, ka, va, qi, ki, wi, qb, kb, vb, ga, gb = jnp.split(z, SPLIT_POINTS, axis=-1)
    qa = rope(qa.reshape(bn, s, A_HEADS, HEAD_DIM), pos)
    ka = rope(ka.reshape(bn, s, A_KV_HEADS, HEAD_DIM), pos)
    va = va.reshape(bn, s, A_KV_HEADS, HEAD_DIM)
    qi = rope(qi.reshape(bn, s, IDX_HEADS, IDX_DIM), pos)
    ki = rope(ki, pos)
    qb = rope(qb.reshape(bn, s, B_HEADS, 2, HEAD_DIM), pos)
    kb = rope(kb.reshape(bn, s, B_HEADS, 2, HEAD_DIM), pos)
    vb = vb.reshape(bn, s, B_HEADS, 2 * HEAD_DIM)
    return qa, ka, va, qi, ki, wi, qb, kb, vb, ga, gb

def dsa_attend(qa, qi, wi, ka, va, ki, valid, topk):
    bn, q = qa.shape[:2]
    s = jnp.einsum('bqhd,bld->bqhl', qi, ki)
    score = jnp.einsum('bqhl,bqh->bql', jax.nn.relu(s), wi).astype(jnp.float32) * IDX_SCALE
    score = jnp.where(valid[None], score, -jnp.inf)
    top_s, top_i = lax.top_k(score, topk)
    sel_ok = jnp.isfinite(top_s)
    kg = jax.vmap(lambda kb_, ib: kb_[ib])(ka, top_i)
    vg = jax.vmap(lambda vb_, ib: vb_[ib])(va, top_i)
    qg = qa.reshape(bn, q, A_KV_HEADS, A_HEADS // A_KV_HEADS, HEAD_DIM)
    logits = jnp.einsum('bqkgd,bqjkd->bqkgj', qg, kg).astype(jnp.float32) * ATTN_SCALE
    logits = jnp.where(sel_ok[:, :, None, None, :], logits, -jnp.inf)
    p = jax.nn.softmax(logits, axis=-1)
    o = jnp.einsum('bqkgj,bqjkd->bqkgd', p.astype(vg.dtype), vg)
    return o.reshape(bn, q, A_WIDTH)

def diff_attend(qb, kb, vb, valid, lam, lam_init):
    bn, q = qb.shape[:2]
    logits = jnp.einsum('bqhcd,blhcd->bhcql', qb, kb).astype(jnp.float32) * ATTN_SCALE
    logits = jnp.where(valid[None, None, None], logits, -jnp.inf)
    p = jax.nn.softmax(logits, axis=-1)
    a = p[:, :, 0] - lam * p[:, :, 1]
    o = jnp.einsum('bhql,blhe->bqhe', a.astype(vb.dtype), vb).astype(jnp.float32)
    o = o * lax.rsqrt(jnp.mean(o * o, axis=-1, keepdims=True) + EPS) * (1.0 - lam_init)
    return o.astype(vb.dtype).reshape(bn, q, B_V_WIDTH)

def mix_prompt(qa, ka, va, qi, ki, wi, qb, kb, vb, lam, lam_init):
    bn, s = qa.shape[:2]
    nb = s // QBLOCK
    topk = min(TOPK_MAX, s // 4)
    k_chunk = jnp.arange(s) // CHUNK

    def blocks(t):
        return jnp.moveaxis(t.reshape((bn, nb, QBLOCK) + t.shape[2:]), 1, 0)

    def body(args):
        blk, qa_b, qi_b, wi_b, qb_b = args
        q_chunk = (blk * QBLOCK + jnp.arange(QBLOCK)) // CHUNK
        valid = k_chunk[None, :] <= q_chunk[:, None]
        oa = dsa_attend(qa_b, qi_b, wi_b, ka, va, ki, valid, topk)
        ob = diff_attend(qb_b, kb, vb, valid, lam, lam_init)
        return oa, ob

    oa, ob = lax.map(body, (jnp.arange(nb), blocks(qa), blocks(qi), blocks(wi), blocks(qb)))
    oa = jnp.moveaxis(oa, 0, 1).reshape(bn, s, A_WIDTH)
    ob = jnp.moveaxis(ob, 0, 1).reshape(bn, s, B_V_WIDTH)
    return oa, ob

def mix_sample(qa, ka, va, qi, ki, wi, qb, kb, vb, caches, lam, lam_init):
    c_ak, c_av, c_ik, c_bk, c_bv = caches
    ka_all = jnp.concatenate([c_ak, ka], axis=1)
    va_all = jnp.concatenate([c_av, va], axis=1)
    ki_all = jnp.concatenate([c_ik, ki], axis=1)
    kb_all = jnp.concatenate([c_bk, kb], axis=1)
    vb_all = jnp.concatenate([c_bv, vb], axis=1)
    q, l = qa.shape[1], ka_all.shape[1]
    valid = jnp.ones((q, l), dtype=bool)
    topk = min(TOPK_MAX, l // 4)
    oa = dsa_attend(qa, qi, wi, ka_all, va_all, ki_all, valid, topk)
    ob = diff_attend(qb, kb_all, vb_all, valid, lam, lam_init)
    return oa, ob

def run_layer(x, c, pos, mixer, w_ada, b_ada, g_pre_mix, g_post_mix, g_pre_ffn, g_post_ffn,
              w_in, w_o_a, w_o_b, w_out, w_gate, w_up, w_down):
    ada = jax.nn.silu(c) @ w_ada + b_ada
    sh1, sc1, gt1, sh2, sc2, gt2 = jnp.split(ada, 6, axis=-1)
    h = modulate(rms_norm(x, g_pre_mix), sh1, sc1)
    qa, ka, va, qi, ki, wi, qb, kb, vb, ga, gb = project(h, pos, w_in)
    oa, ob = mixer(qa, ka, va, qi, ki, wi, qb, kb, vb)
    m = jax.nn.sigmoid(ga) * (oa @ w_o_a) + jax.nn.sigmoid(gb) * (ob @ w_o_b)
    x = x + gt1[:, None] * rms_norm(m @ w_out, g_post_mix)
    h = modulate(rms_norm(x, g_pre_ffn), sh2, sc2)
    f = (jax.nn.silu(h @ w_gate) * (h @ w_up)) @ w_down
    x = x + gt2[:, None] * rms_norm(f, g_post_ffn)
    return x, (ka, va, ki, kb, vb)

def setup_inputs(seed: int = 0) -> dict:
    key = jax.random.key(seed)
    ks = jax.random.split(key, 32)
    D = D_MODEL

    def nrm(k, shape, scale):
        return jax.random.normal(k, shape, jnp.float32) * scale

    return {
        'x_prompt': nrm(ks[0], (BATCH, SEQ, D), 1.0),
        'x_sample': nrm(ks[1], (DEC_BATCH, DEC_SEQ, D), 1.0),
        'cache_a_k': nrm(ks[2], (DEPTH, DEC_BATCH, PAST_LEN, A_KV_HEADS, HEAD_DIM), 1.0),
        'cache_a_v': nrm(ks[3], (DEPTH, DEC_BATCH, PAST_LEN, A_KV_HEADS, HEAD_DIM), 1.0),
        'cache_idx_k': nrm(ks[4], (DEPTH, DEC_BATCH, PAST_LEN, IDX_DIM), 1.0),
        'cache_b_k': nrm(ks[5], (DEPTH, DEC_BATCH, PAST_LEN, B_HEADS, 2, HEAD_DIM), 1.0),
        'cache_b_v': nrm(ks[6], (DEPTH, DEC_BATCH, PAST_LEN, B_HEADS, 2 * HEAD_DIM), 1.0),
        'c_prompt': nrm(ks[7], (BATCH, D), 1.0),
        'c_sample': nrm(ks[8], (DEC_BATCH, D), 1.0),
        'w_ada': nrm(ks[9], (DEPTH, D, 6 * D), 0.5 * D ** -0.5),
        'b_ada': nrm(ks[10], (DEPTH, 6 * D), 0.02),
        'g_pre_mix': 1.0 + nrm(ks[11], (DEPTH, D), 0.05),
        'g_post_mix': 1.0 + nrm(ks[12], (DEPTH, D), 0.05),
        'g_pre_ffn': 1.0 + nrm(ks[13], (DEPTH, D), 0.05),
        'g_post_ffn': 1.0 + nrm(ks[14], (DEPTH, D), 0.05),
        'w_in': nrm(ks[15], (DEPTH, D, IN_COLS), D ** -0.5),
        'lam_q1': nrm(ks[16], (DEPTH, HEAD_DIM), 0.1),
        'lam_k1': nrm(ks[17], (DEPTH, HEAD_DIM), 0.1),
        'lam_q2': nrm(ks[18], (DEPTH, HEAD_DIM), 0.1),
        'lam_k2': nrm(ks[19], (DEPTH, HEAD_DIM), 0.1),
        'w_o_a': nrm(ks[20], (DEPTH, A_WIDTH, D), A_WIDTH ** -0.5),
        'w_o_b': nrm(ks[21], (DEPTH, B_V_WIDTH, D), B_V_WIDTH ** -0.5),
        'w_out': nrm(ks[22], (DEPTH, D, D), D ** -0.5),
        'w_gate': nrm(ks[23], (DEPTH, D, D_FF), D ** -0.5),
        'w_up': nrm(ks[24], (DEPTH, D, D_FF), D ** -0.5),
        'w_down': nrm(ks[25], (DEPTH, D_FF, D), D_FF ** -0.5),
    }

def reference(x_prompt, x_sample, cache_a_k, cache_a_v, cache_idx_k, cache_b_k, cache_b_v,
              c_prompt, c_sample, w_ada, b_ada, g_pre_mix, g_post_mix, g_pre_ffn, g_post_ffn,
              w_in, lam_q1, lam_k1, lam_q2, lam_k2, w_o_a, w_o_b, w_out, w_gate, w_up, w_down):
    pos_p = jnp.arange(x_prompt.shape[1])
    pos_s = cache_a_k.shape[2] + jnp.arange(x_sample.shape[1])
    yp, ys = x_prompt, x_sample
    rows_p, rows_s = [], []
    for l in range(DEPTH):
        lam_init = 0.8 - 0.6 * math.exp(-0.3 * l)
        lam = (jnp.exp(jnp.sum(lam_q1[l].astype(jnp.float32) * lam_k1[l].astype(jnp.float32)))
               - jnp.exp(jnp.sum(lam_q2[l].astype(jnp.float32) * lam_k2[l].astype(jnp.float32)))
               + lam_init)
        caches_l = (cache_a_k[l], cache_a_v[l], cache_idx_k[l], cache_b_k[l], cache_b_v[l])
        lw = (w_ada[l], b_ada[l], g_pre_mix[l], g_post_mix[l], g_pre_ffn[l], g_post_ffn[l],
              w_in[l], w_o_a[l], w_o_b[l], w_out[l], w_gate[l], w_up[l], w_down[l])
        prompt_mix = functools.partial(mix_prompt, lam=lam, lam_init=lam_init)
        sample_mix = functools.partial(mix_sample, caches=caches_l, lam=lam, lam_init=lam_init)
        yp, rp = run_layer(yp, c_prompt, pos_p, prompt_mix, *lw)
        ys, rs = run_layer(ys, c_sample, pos_s, sample_mix, *lw)
        rows_p.append(rp)
        rows_s.append(rs)

    def stack(rows, i):
        return jnp.stack([r[i] for r in rows], axis=0)

    return (yp, ys,
            stack(rows_p, 0), stack(rows_p, 1), stack(rows_p, 2), stack(rows_p, 3), stack(rows_p, 4),
            stack(rows_s, 0), stack(rows_s, 1), stack(rows_s, 2), stack(rows_s, 3), stack(rows_s, 4))


_drawn_inputs = setup_inputs


def setup_inputs(seed=0):
    import zlib

    import numpy as np

    out = dict(_drawn_inputs(seed))
    spreads = {}
    factors = {'g_post_mix': 3.707, 'g_pre_ffn': 2.902, 'g_post_ffn': 3.882}
    for name, (base, spread) in spreads.items():
        noise = np.random.default_rng([zlib.crc32(name.encode()), seed]).standard_normal(out[name].shape)
        drawn = base * np.exp(spread * noise) if base else spread * noise
        out[name] = __import__('jax').numpy.asarray(drawn.astype(out[name].dtype))
    for name, factor in factors.items():
        out[name] = (out[name] * factor).astype(out[name].dtype)
    return out
```

```python
import math
from contextlib import ExitStack

import numpy as np
import concourse.bass as bass
from concourse import mybir

F32 = mybir.dt.float32
F32R = mybir.dt.float32r
ALU = mybir.AluOpType
ACT = mybir.ActivationFunctionType
AX = mybir.AxisListType

P = 128
D = 1024
KC = D // P
NS, NP_ = 64, 512
T = NS + NP_
HALF = T // 2
PAST = 256
KEYS = PAST + T
HD = 64
FF = 2816
FC = FF // P
AW, AKV, IQ, IH = 512, 128, 512, 8
BW = 512
TOPK_P, TOPK_S = min(256, NP_ // 4), min(256, (PAST + NS) // 4)
VW = AKV + BW
VWI = VW + IH
VH = VWI // 2
EPS = 1e-6
SCALE = HD ** -0.5
IDX_SCALE = (IH * HD) ** -0.5
LAM_INIT = 0.8 - 0.6 * math.exp(-0.3 * 0)
OUT_OF_REACH = -2e38
TAKEN = -3e38
NEG = -1e30
BLK_DOWN = FC // 2

QCOL = [0] + [NS + P * i for i in range(4)]
KCOL = [0] + [PAST + NS] * 4
NKEY = [PAST + NS, P, 2 * P, 3 * P, 4 * P]
NMOV = [max(n, 256) for n in NKEY]
NBLK = [-(-n // P) for n in NKEY]
VBLK = [0, 3, 3, 3, 3]
QUSE = [NS, P, P, P, P]
ROUNDS = [TOPK_S // 8, 0] + [TOPK_P // 8] * 3
MBOFF = [sum(NKEY[:i]) for i in range(5)]
NG = 8
NU = NG * 5


def plan():
    ch = [("ada", n, q) for n in range(4) for q in range(4)]
    ch += [("ki", 0)] + [("qi", j) for j in range(4)]
    ch += [("v", k) for k in range(KC)]
    for h in range(4):
        ch += [("kb", h), ("qb", h)]
    ch += [("ka", 0)] + [("qa", j) for j in range(4)]
    for d in range(KC):
        ch += [("ga", d), ("gb", d)] + [("ada", 4 + d, q) for q in range(4)] + [("wo", d)]
    return ch


CH = plan()
C_OUT = len(CH)
C_GU = C_OUT + KC
C_DN = C_GU + 2 * FC
AT = {c: i for i, c in enumerate(CH)}
C_V = AT[("v", 0)]
N_ADA0 = 16
ROPES = [c for c in CH if c[0] in ("ki", "qi", "kb", "qb", "ka", "qa")]
ROPE_AT = {c: i for i, c in enumerate(ROPES)}
KTILES = [c for c in ROPES if c[0][0] == "k"]
KT_AT = {c: i for i, c in enumerate(KTILES)}
N_KI = ROPE_AT[("qi", 3)] + 1


def ring(c):
    return c if c < C_V else c - KC


def schedule():
    s = []
    for c in ROPES[:N_KI]:
        s += [("part", AT[c], 0, KC), ("end", AT[c])]
    s += [("vload",)]
    rounds = [(t, r) for t in (4, 3, 2, 0) for r in range(ROUNDS[t])]
    order = [4, 3, 2, 0, 1]
    for n, t in enumerate(order):
        s += [("v", n, t)]
        if t != 1:
            s += [("idx", t, h) for h in range(IH)] + [("idxmask", t)]
        if n >= 0:
            k = 5 if n < 4 else 8
            s += [("topk",) + r for r in rounds[:k]]
            rounds = rounds[k:]
    for c in (("kb", 0), ("qb", 0)):
        s += [("part", AT[c], 0, KC), ("end", AT[c])]
        s += [("topk",) + r for r in rounds[:2]]
        rounds = rounds[2:]
    fill = []
    for g in range(NG):
        nxt = {0: [("kb", 1), ("qb", 1)], 1: [("kb", 2), ("qb", 2)], 2: [("kb", 3), ("qb", 3)],
               3: [("ka", 0), ("qa", 0)], 4: [("qa", 1)], 5: [("qa", 2)], 6: [("qa", 3)], 7: []}[g]
        nb = KC * len(nxt)
        fill = [(AT[c], k) for c in nxt for k in range(KC)]
        for t in range(5):
            u = 5 * g + t
            mine = fill[nb * t // 5:nb * (t + 1) // 5]
            if u:
                s += [("comb", u - 1)]
            s += [("qk", u)]
            cut = [mine[:len(mine) * 2 // 3], mine[len(mine) * 2 // 3:]]
            for part, what in zip(cut, (("tr", u - 1), ("pv", u - 1))):
                for c, k in part:
                    s += [("part", c, k, k + 1)] + ([("end", c)] if k == KC - 1 else [])
                if u:
                    s += [what]
            k = 2 if g < 3 else len(rounds)
            s += [("topk",) + r for r in rounds[:k]]
            rounds = rounds[k:]
            if u == 20:
                s += [("bnorm",)]
    s += [("comb", NU - 1), ("tr", NU - 1), ("pv", NU - 1), ("flush",)]
    assert not rounds
    return s


def transposes_before(u):
    return u if u <= 20 else 20 + 2 * (u - 20)


def build(nc, a, o):
    with ExitStack() as ctx:
        base = -(-nc.sbuf_base // 64) * 64
        at = {"x": base}

        def sb(name, shape, dt=F32, where=None):
            n = int(np.prod(shape[1:])) * 4
            off = where
            if where is None:
                off = at["x"]
                at["x"] += -(-n // 32) * 32
            assert off + n <= nc.sbuf_usable_end, name
            return nc.alloc_sbuf_tensor_at(name, shape, dt, offset=off), off + n

        cos, _ = sb("cos", [P, T])
        sin, _ = sb("sin", [P, T])
        off_cos, off_sin = base, base + T * 4
        off_cs = at["x"]
        cstat, _ = sb("cstat", [P, KC, P], F32R)
        ident, _ = sb("ident", [P, P])
        ones, _ = sb("ones", [P, P])
        ada, _ = sb("ada", [P, 48, 2])
        bada, _ = sb("bada", [P, 48, 2])
        gains, _ = sb("gains", [P, 4, KC])
        gs, _ = sb("gs", [P, 2, KC, 2])
        gg, _ = sb("gg", [P, 2, KC, 2])
        ct, _ = sb("ct", [P, KC, 2])
        cf, _ = sb("cf", [P, KC, 2])
        hmask, _ = sb("hmask", [P, 2])
        wis, _ = sb("wis", [P, 5, IH])
        lam, _ = sb("lam", [P, 3])
        eps, _ = sb("eps", [P, 1])
        mx, _ = sb("mx", [P, NU, 2])
        nmx, _ = sb("nmx", [P, NU, 2])
        esum, _ = sb("esum", [P, NU, 2])
        rsum, _ = sb("rsum", [P, NU, 2])
        nlr, _ = sb("nlr", [P, 20])
        osq, _ = sb("osq", [P, 20])
        orms, _ = sb("orms", [P, 20])
        top8, _ = sb("top8", [P, 8])
        t4, _ = sb("t4", [P, 4, 4])
        raw_off = at["x"]
        raw, _ = sb("raw", [P, 4, 1024])
        rawd, _ = sb("rawd", [P, 2, BLK_DOWN * P], where=raw_off)
        whi, _ = sb("whi", [P, 2, BLK_DOWN * P], F32R)
        wlo, _ = sb("wlo", [P, 2, BLK_DOWN * P], F32R)
        h_off = at["x"]
        hh, e1 = sb("hh", [P, KC, T], F32R)
        hl, _ = sb("hl", [P, KC, T], F32R)
        ymix, _ = sb("ymix", [P, KC, T], where=h_off)
        xres, _ = sb("xres", [P, KC, T], where=h_off + KC * T * 4)
        A0 = at["x"]
        A1 = A0 + KC * T * 4 * 1 + 2 * FC * T * 4
        assert A1 <= nc.sbuf_usable_end, (A1, nc.sbuf_usable_end)
        qi_h, n = sb("qi_h", [P, 4, T], F32R, A0)
        qi_l, n = sb("qi_l", [P, 4, T], F32R, n)
        oT, _ = sb("oT", [P, KC, T], F32, A0)
        ki, e = sb("ki", [P, 2, 2, KEYS], F32R, n)
        ob, _ = sb("ob", [P, 20, P], F32, n)
        kz0, n = sb("kz0", [P, 2, 2, KEYS], F32R, e)
        kz1, n = sb("kz1", [P, 2, 2, KEYS], F32R, n)
        q0, n = sb("q0", [P, 2, T], F32R, n)
        q1, n = sb("q1", [P, 2, T], F32R, n)
        pt, pe_ = sb("pt", [P, 2, 512], F32, n)
        wv_h, n = sb("wv_h", [P, KC, VWI], F32R, e)
        wv_l, n = sb("wv_l", [P, KC, VWI], F32R, n)
        n = max(n, pe_)
        v_off = n
        vt, n = sb("vt", [P, 7, VWI], F32, n)
        mb, n = sb("mb", [P, MBOFF[4] + NKEY[4]], F32, n)
        e_off = n
        ee, n = sb("ee", [P, 2, 2, 512], F32, n)
        z, n = sb("z", [P, T], F32, n)
        zc, n = sb("zc", [P, T], F32, n)
        zs, n = sb("zs", [P, T], F32, n)
        ro, n = sb("ro", [P, 2, KEYS], F32, n)
        on, n = sb("on", [P, P], F32, n)
        assert n <= nc.sbuf_usable_end, n
        xt, n = sb("xt", [P, KC, T], F32, v_off)
        rowa, n = sb("rowa", [P, 512], F32, n)
        lamv, n = sb("lamv", [P, 4, HD], F32, n)
        sq0, n = sb("sq0", [P, 2, T], F32, n)
        xr0, n = sb("xr0", [P, 2, T], F32, n)
        hf0, n = sb("hf0", [P, 2, T], F32, A0)
        rstd0, n2 = sb("rstd0", [P, T], F32, n)
        rms0, n = sb("rms0", [P, T], F32, n)
        assert n2 <= nc.sbuf_usable_end
        oth, n = sb("oth", [P, KC, T], F32R, A0 + KC * T * 4)
        otl, n = sb("otl", [P, KC, T], F32R, n)
        mh, n = sb("mh", [P, KC, T], F32R, n)
        ml, n = sb("ml", [P, KC, T], F32R, n)
        sga, n = sb("sga", [P, T], F32, n)
        sgb, n = sb("sgb", [P, T], F32, n)
        mt, n = sb("mt", [P, T], F32, n)
        rowb, n = sb("rowb", [P, 512], F32, n)
        assert n <= nc.sbuf_usable_end, n
        x1, n = sb("x1", [P, KC, T], F32, A0)
        sq1, n = sb("sq1", [P, 2, T], F32, n)
        xr1, n = sb("xr1", [P, 2, T], F32, n)
        hf1, n = sb("hf1", [P, 2, T], F32, n)
        rstd1, n = sb("rstd1", [P, T], F32, n)
        rms1, n = sb("rms1", [P, T], F32, n)
        rstd2, n = sb("rstd2", [P, T], F32, n)
        acc1, _ = sb("acc1", [P, T], F32, off_cs)
        acc2, _ = sb("acc2", [P, T], F32, off_cs)
        fh, n = sb("fh", [P, FC, T], F32R, A0 + KC * T * 4)
        fl, n = sb("fl", [P, FC, T], F32R, n)
        assert n <= A1
        ft, _ = sb("ft", [P, T], F32, off_cos)
        sg, _ = sb("sg", [P, T], F32, off_sin)
        sq2, _ = sb("sq2", [P, T], F32, off_cos)
        rstd3, _ = sb("rstd3", [P, T], F32, off_sin)
        hh2 = nc.alloc_sbuf_tensor_at("hh2", [P, KC, T], F32R, offset=h_off)
        hl2 = nc.alloc_sbuf_tensor_at("hl2", [P, KC, T], F32R, offset=h_off + KC * T * 4)

        def pb(name, shape):
            return ctx.enter_context(nc.psum_tensor(name, shape, F32))

        pj = [pb("pj0", [P, 2, 512]), pb("pj1", [P, 2, 512])]
        lg = pb("lg", [P, 2, 512])
        tb = pb("tb", [P, 512])
        pvb = pb("pvb", [P, 512])

        def sem(name):
            return ctx.enter_context(nc.semaphore(name))

        const_in = sem("const_in")
        xres_in = sem("xres_in")
        raw_in = [sem(f"raw_in{i}") for i in range(4)]
        down_in = [sem(f"down_in{i}") for i in range(2)]
        cache_in = [sem(f"cache_in{i}") for i in range(len(KTILES))]
        k_out = [sem(f"k_out{i}") for i in range(len(KTILES))]
        vp_out, vs_out = sem("vp_out"), sem("vs_out")
        y_out = sem("y_out")
        w_hi = sem("w_hi")
        w_lo = sem("w_lo")
        w_lo_dve = sem("w_lo_dve")
        ada_used = sem("ada_used")
        down_used = sem("down_used")
        pj_full = sem("pj_full")
        pj_act = sem("pj_act")
        pj_dve = sem("pj_dve")
        consts = sem("consts")
        c_silu, c_hi, c_lo = sem("c_silu"), sem("c_hi"), sem("c_lo")
        ada_sb, ada_cols, ada_done = sem("ada_sb"), sem("ada_cols"), sem("ada_done")
        sq_ready, sq_used, rms_ready, rstd_ready = (sem("sq_ready"), sem("sq_used"), sem("rms_ready"),
                                                    sem("rstd_ready"))
        xr_ready, hf_ready, h_hi, h_lo = sem("xr_ready"), sem("hf_ready"), sem("h_hi"), sem("h_lo")
        z_ready, zc_ready, rope_o, rope_hi, rope_lo = (sem("z_ready"), sem("zc_ready"), sem("rope_o"),
                                                       sem("rope_hi"), sem("rope_lo"))
        dve = sem("dve")
        v_ready, wi_ready = sem("v_ready"), sem("wi_ready")
        ix_full, ix_relu, ix_acc = sem("ix_full"), sem("ix_relu"), sem("ix_acc")
        lam_dots, lam_exp = sem("lam_dots"), sem("lam_exp")
        qk_ready, mx_ready, e_ready, p_ready = sem("qk_ready"), sem("mx_ready"), sem("e_ready"), sem("p_ready")
        tr_ready, pt_ready, pt_used, pv_ready, o_ready = (sem("tr_ready"), sem("pt_ready"), sem("pt_used"),
                                                          sem("pv_ready"), sem("o_ready"))
        oT_full, oT_done = sem("oT_full"), sem("oT_done")
        on_rms, on_ready = sem("on_rms"), sem("on_ready")
        ob_full, ob_done = sem("ob_full"), sem("ob_done")
        ot_hi, ot_lo = sem("ot_hi"), sem("ot_lo")
        m_ready, m_hi, m_lo = sem("m_ready"), sem("m_hi"), sem("m_lo")
        y_ready, ysq_ready, acc_ready, acc_zero = (sem("y_ready"), sem("ysq_ready"), sem("acc_ready"),
                                                   sem("acc_zero"))
        yg_ready, x1_dve, x1_pool = sem("yg_ready"), sem("x1_dve"), sem("x1_pool")
        f_hi, f_lo = sem("f_hi"), sem("f_lo")
        y_fin = sem("y_fin")

        SCHED = schedule()

        takers = []
        tile_of = {}
        for n in range(1):
            tile_of["stat0"] = len(takers); takers.append("A")
        for s in SCHED:
            if s[0] == "end":
                tile_of[s[1]] = len(takers); takers.append("A")
            if s[0] == "v":
                tile_of[("v", s[2])] = len(takers); takers.append("A")
        for d in range(KC):
            for k, who in (("ga", "A"), ("gb", "A"), ("oa", "D"), ("ob", "D")):
                tile_of[(k, d)] = len(takers)
                if k in ("ga", "gb"):
                    tile_of[AT[(k, d)]] = len(takers)
                takers.append(who)
        T_OUT = len(takers)
        takers += ["A"] * KC
        tile_of["stat1"] = len(takers); takers.append("A")
        tile_of["stat2"] = len(takers); takers.append("A")
        T_GU = len(takers)
        takers += ["A", "D"] * FC
        T_DN = len(takers)
        takers += ["A"] * KC
        tile_of["stat3"] = len(takers); takers.append("A")

        def taken(n, who):
            return takers[:n + 1].count(who)

        def pj_free(pe, n):
            if n >= 2:
                who = takers[n - 2]
                pe.wait_ge(pj_act if who == "A" else pj_dve, taken(n - 2, who))

        def two(ap):
            return ap.rearrange("p (a b) -> p a b", a=2)

        def pj_view(n):
            return pj[n % 2][:, :, 0:HALF]

        def in_dve(c):
            return c < N_ADA0

        def lo_count(c):
            return c + 1 - N_ADA0

        def wait_lo(eng, c):
            if in_dve(c):
                eng.wait_ge(w_lo_dve, c + 1)
            else:
                eng.wait_ge(w_lo, lo_count(c))

        def sem_of_raw(eng, c):
            eng.wait_ge(raw_in[c % 4], 16 * (c // 4 + 1))

        def wait_used(eng, c, turns=None, chunks=0):
            if c >= C_DN:
                d, k = divmod(c - C_DN, 2)
                if k == 0:
                    eng.wait_ge(down_used, d + 1)
                    return
                tile = T_DN + d
            elif c >= C_GU:
                tile = T_GU + c - C_GU
            elif c >= C_OUT:
                tile = T_OUT + c - C_OUT
            elif CH[c][0] == "ada":
                eng.wait_ge(ada_used, sum(x[0] == "ada" for x in CH[:c + 1]))
                return
            elif CH[c][0] == "wo":
                tile = tile_of[("ob", CH[c][1])]
            else:
                tile = tile_of[c]
            eng.wait_ge(pj_full, tile + 1 if turns is None else turns * chunks + (tile + 1))

        def slot_free(eng, c):
            if ring(c) >= 2:
                before = c - 2 if not C_V + KC <= c < C_V + KC + 2 else c - KC - 2
                wait_used(eng, before)

        def kz_of(c):
            name, j = c
            return ki if name == "ki" else (kz1 if name == "kb" and j % 2 else kz0)

        def q_of(c):
            name, j = c
            if name == "qi":
                return qi_h[:, j, :], qi_l[:, j, :]
            t = q1 if j % 2 else q0
            return t[:, 0, :], t[:, 1, :]

        def rope_dst_free(eng, c):
            name, j = c
            if name == "kb":
                if j < 2:
                    eng.wait_ge(pj_full, tile_of[("v", 1)] + 1)
                else:
                    eng.wait_ge(qk_ready, 5 * (j - 1))
            elif name == "qb":
                if j >= 2:
                    eng.wait_ge(qk_ready, 5 * (j - 1))
            elif name == "ka":
                eng.wait_ge(qk_ready, 15)
            elif name == "qa":
                eng.wait_ge(qk_ready, 5 * (3 + j))

        def unit(u):
            g, t = divmod(u, 5)
            return g, t, g < 4

        def wait_set_used(eng, n):
            if n < 20:
                eng.wait_ge(pv_ready, n + 1)
            elif n % 2:
                eng.wait_ge(pv_ready, 20 + (n - 20) // 2 + 1)
            else:
                eng.wait_ge(pt_used, (n - 20) // 2 + 1)

        def last_rope(g):
            return ROPE_AT[("qb", g)] if g < 4 else ROPE_AT[("qa", g - 4)]

        block = ctx.enter_context(nc.Block())

        @block.sync
        def _(sp):
            def load(c):
                if c >= 4:
                    wait_lo(sp, c - 4)
                name = CH[c]
                if name[0] == "v":
                    dst, src = raw[:, c % 4, 0:VWI], a["w_v"][name[1]]
                elif name[0] == "ada":
                    dst, src = raw[:, c % 4, :], a["w_ada"][name[1] * 4 + name[2]]
                else:
                    row = W_ROW[name]
                    dst, src = raw[:, c % 4, :], a["w_s"][row]
                sp.dma_start(dst, src).then_inc(raw_in[c % 4], 16)

            sp.dma_start(ct[:, :, :], a["cT"]).then_inc(const_in, 16)
            load(0)
            load(1)
            for dst, src in ((xt, "xT"), (ident, "ident"), (cos, "cos"), (sin, "sin"), (gains, "gains"),
                             (bada, "bada"), (hmask, "hmask"), (lamv, "lamv")):
                sp.dma_start(dst[...], a[src]).then_inc(const_in, 16)
            for c in range(2, C_OUT):
                load(c)
                if c >= 2 and CH[c - 1] in KT_AT:
                    k = CH[c - 1]
                    r = ROPE_AT[k]
                    if r == 0:
                        sp.wait_ge(h_lo, KC)
                    if r >= 2:
                        sp.wait_ge(rope_hi, r - 1)
                        sp.wait_ge(rope_lo, r - 1)
                        if ROPES[r - 2] in KT_AT:
                            sp.wait_ge(k_out[KT_AT[ROPES[r - 2]]], 16)
                    sp.dma_start(ro[:, r % 2, 0:PAST], a["cache_k"][KT_AT[k]]).then_inc(cache_in[KT_AT[k]], 16)
                if c == C_V:
                    sp.wait_ge(h_lo, KC)
                    sp.dma_start(vt[:, 0:2, 0:VW], a["cache_v"]).then_inc(const_in, 16)
            for c in range(C_OUT, C_OUT + 4):
                wait_lo(sp, c - 4)
                sp.dma_start(raw[:, c % 4, :], a["w_s"][S_OUT + c - C_OUT]).then_inc(raw_in[c % 4], 16)
            wait_used(sp, AT[("gb", KC - 1)])
            sp.dma_start(xres[:, :, :], a["xT"]).then_inc(xres_in, 16)
            with sp.Fori(0, (C_DN - C_OUT - 4) // 4) as i:
                for k in range(4):
                    c = C_OUT + 4 + k
                    sp.wait_ge(w_lo, i * 4 + lo_count(c - 4))
                    sp.dma_start(raw[:, c % 4, :], a["w_s"][bass.ds(i * 4 + (S_OUT + 4 + k), 1)]
                                 .rearrange("a p n -> p (a n)")).then_inc(raw_in[c % 4], 16)
            sp.wait_ge(w_lo, lo_count(C_DN - 1))
            for k in range(2):
                sp.dma_start(rawd[:, k, :], a["w_d"][k]).then_inc(down_in[k], 16)
            with sp.Fori(0, KC - 1) as i:
                for k in range(2):
                    sp.wait_ge(w_lo, i * 2 + (lo_count(C_DN + k)))
                    sp.dma_start(rawd[:, k, :], a["w_d"][bass.ds(i * 2 + (2 + k), 1)]
                                 .rearrange("a p n -> p (a n)")).then_inc(down_in[k], 16)
            for kc in range(KC):
                sp.wait_ge(y_fin, kc + 1)
                sp.dma_start(o["yT"][kc], x1[:, kc, :]).then_inc(y_out, 16)
            sp.wait_ge(y_out, 16 * KC)
            sp.wait_ge(vp_out, 16)
            sp.wait_ge(vs_out, 16)
            for s in k_out:
                sp.wait_ge(s, 16)

        @block.scalar
        def _(act):
            def hi(c):
                sem_of_raw(act, c)
                name = CH[c] if c < C_OUT else None
                if name and name[0] == "v":
                    dst, src = wv_h[:, name[1], :], raw[:, c % 4, 0:VWI]
                else:
                    slot_free(act, c)
                    dst, src = whi[:, ring(c) % 2, 0:1024], raw[:, c % 4, :]
                act.activation(dst, src, ACT.Copy).then_inc(w_hi, 1)

            act.wait_ge(const_in, 16 * 9)
            act.activation(cf[:, :, :], ct[:, :, :], ACT.Silu).then_inc(c_silu, 1)
            act.wait_ge(consts, 3)
            act.wait_ge(c_silu, 1)
            act.activation(cstat[:, :, 0:2], cf[:, :, :], ACT.Copy).then_inc(c_hi, 1)
            hi(0)
            hi(1)

            def rows(n, dst):
                act.wait_ge(ada_used, 4 * (n + 1))
                if n >= 1:
                    act.wait_ge(ada_cols, n)
                act.activation(dst[0:4, :], tb[0:4, :], ACT.Copy).then_inc(ada_sb, 1)

            def squares(src, sq, first):
                for kc in range(KC):
                    if first + kc >= 2:
                        act.wait_ge(sq_used, first + kc - 1)
                    act.activation(sq[:, kc % 2, :], src[:, kc, :], ACT.Square).then_inc(sq_ready, 1)

            def rms(tile, dst, n):
                act.wait_ge(pj_full, tile + 1)
                act.wait_ge(consts, 3)
                act.activation(two(dst[:, :]), pj_view(tile), ACT.Sqrt, bias=eps[:, 0:1], scale=1.0 / D)\
                   .then_inc(pj_act, 1)

            squares(xt, sq0, 0)
            for c in range(N_ADA0):
                if c + 2 < N_ADA0:
                    hi(c + 2)
                if c % 4 == 3:
                    rows(c // 4, rowa)
                if c == 11:
                    rms(tile_of["stat0"], rms0, 0)
            hi(N_ADA0)
            hi(N_ADA0 + 1)
            for kc in range(KC):
                act.wait_ge(hf_ready, kc + 1)
                act.activation(hh[:, kc, :], hf0[:, kc % 2, :], ACT.Copy).then_inc(h_hi, 1)
            act.wait_ge(lam_dots, 1)
            act.activation(lam[:, 0:2], lam[:, 0:2], ACT.Exp).then_inc(lam_exp, 1)

            def rope_evac(c):
                n, r = tile_of[c], ROPE_AT[CH[c]]
                act.wait_ge(pj_full, n + 1)
                if r == 0:
                    act.wait_ge(h_lo, KC)
                if r >= 1:
                    act.wait_ge(rope_o, r)
                act.activation(two(z[:, :]), pj_view(n), ACT.Copy).then_inc(pj_act, 1)

            def rope_split(c):
                name = CH[c]
                r = ROPE_AT[name]
                act.wait_ge(rope_o, r + 1)
                rope_dst_free(act, name)
                if name in KT_AT:
                    k = KT_AT[name]
                    act.dma_start(o["kT"][k], ro[:, r % 2, PAST:KEYS]).then_inc(k_out[k], 16)
                    act.wait_ge(cache_in[k], 16)
                    dst = kz_of(name)
                    for m in range(2):
                        ins = act.activation(dst[:, 0, m, :], ro[:, r % 2, :], ACT.Copy, scale=hmask[:, m:m + 1])
                    ins.then_inc(rope_hi, 1)
                else:
                    act.activation(q_of(name)[0], ro[:, r % 2, PAST:KEYS], ACT.Copy).then_inc(rope_hi, 1)

            ix = 0
            sets = 0
            for s in SCHED:
                if s[0] == "end":
                    c = s[1]
                    rope_evac(c)
                    nxt = c + 2
                    if nxt < C_V or (c >= C_V and nxt < C_OUT):
                        hi(nxt)
                    rope_split(c)
                elif s[0] == "vload":
                    for k in range(KC + 2):
                        hi(C_V + k)
                elif s[0] == "v":
                    n, t = s[1], s[2]
                    act.wait_ge(pj_full, tile_of[("v", t)] + 1)
                    blk = 2 if t == 0 else 2 + t
                    act.activation(two(vt[:, blk, :]), pj[tile_of[("v", t)] % 2][:, :, 0:VH], ACT.Copy)\
                       .then_inc(pj_act, 1)
                    act.wait_ge(pj_act, taken(tile_of[("v", t)], "A"))
                    if t == 0:
                        act.dma_start(o["v_s"], vt[0:NS, 2, 0:VW]).then_inc(vs_out, 16)
                elif s[0] == "idx":
                    t = s[1]
                    act.wait_ge(ix_full, ix + 1)
                    if ix >= 2:
                        act.wait_ge(ix_acc, ix - 1)
                    act.activation(ee[:, 0, ix % 2, 0:NKEY[t]], lg[:, ix % 2, 0:NKEY[t]], ACT.Relu)\
                       .then_inc(ix_relu, 1)
                    ix += 1
                elif s[0] == "qk":
                    u = s[1]
                    g, t, diff = unit(u)
                    if u == 0:
                        act.wait_ge(ix_acc, 32)
                    act.wait_ge(mx_ready, u + 1)
                    for m in range(2):
                        src = lg[:, m, 0:NKEY[t]] if diff else ee[:, u % 2, m, 0:NKEY[t]]
                        ins = act.activation(ee[:, u % 2, m, 0:NKEY[t]], src, ACT.Exp, bias=nmx[:, u, m:m + 1],
                                             scale=SCALE, accum_out=esum[:, u, m:m + 1])
                    ins.then_inc(e_ready, 1)
                elif s[0] == "tr":
                    g, t, diff = unit(s[1])
                    for m in range(1 if diff else 2):
                        act.wait_ge(tr_ready, sets + 1)
                        if sets >= 2:
                            wait_set_used(act, sets - 2)
                        act.activation(pt[:, sets % 2, 0:NBLK[t] * P], tb[:, 0:NBLK[t] * P], ACT.Copy)\
                           .then_inc(pt_ready, 1)
                        sets += 1
                elif s[0] == "bnorm":
                    act.wait_ge(o_ready, 20)
                    act.activation(orms[:, :], osq[:, :], ACT.Sqrt, bias=eps[:, 0:1], scale=1.0 / P)\
                       .then_inc(on_rms, 1)
            act.wait_ge(oT_done, 20)
            act.wait_ge(ob_done, 5)
            for out_sem in (vp_out, vs_out, *k_out):
                act.wait_ge(out_sem, 16)
            for kc in range(KC):
                act.activation(oth[:, kc, :], oT[:, kc, :], ACT.Copy).then_inc(ot_hi, 1)
            c = AT[("ga", 0)]
            for d in range(KC):
                for q, name in enumerate(("ga", "gb")):
                    n = tile_of[(name, d)]
                    act.wait_ge(pj_full, n + 1)
                    if d:
                        act.wait_ge(m_ready, d)
                    act.activation(two((sga, sgb)[q][:, :]), pj_view(n), ACT.Sigmoid).then_inc(pj_act, 1)
                    hi(c + 2)
                    c += 1
                for q in range(4):
                    hi(c + 2)
                    c += 1
                rows(4 + d, rowb)
                if c + 2 < C_OUT + 2:
                    hi(c + 2)
                    c += 1
                act.wait_ge(m_ready, d + 1)
                act.activation(mh[:, d, :], mt[:, :], ACT.Copy).then_inc(m_hi, 1)
            for d in range(KC):
                n = T_OUT + d
                act.wait_ge(pj_full, n + 1)
                if d == 0:
                    wait_used(act, AT[("gb", KC - 1)])
                act.activation(two(ymix[:, d, :]), pj_view(n), ACT.Copy).then_inc(pj_act, 1)
                hi(C_OUT + d + 2)
                if d >= 2:
                    act.wait_ge(acc_ready, d - 1)
                act.wait_ge(pj_act, taken(n, "A"))
                if d == 0:
                    wait_used(act, C_OUT - 1)
                act.activation(sq1[:, d % 2, :], ymix[:, d, :], ACT.Square).then_inc(ysq_ready, 1)
            act.wait_ge(consts, 3)
            rms(tile_of["stat1"], rms1, 1)
            for kc in range(KC):
                if kc % 2:
                    act.wait_ge(x1_dve, kc // 2 + 1)
                else:
                    act.wait_ge(x1_pool, kc // 2 + 1)
                if kc < 2:
                    act.wait_ge(acc_ready, KC)
                else:
                    act.wait_ge(sq_used, KC - 1 + kc - 1)
                act.activation(sq1[:, kc % 2, :], x1[:, kc, :], ACT.Square).then_inc(sq_ready, 1)
            act.wait_ge(rstd_ready, 2)
            rms(tile_of["stat2"], rms1, 2)
            for kc in range(KC):
                act.wait_ge(hf_ready, KC + kc + 1)
                act.activation(hh2[:, kc, :], hf1[:, kc % 2, :], ACT.Copy).then_inc(h_hi, 1)
            def gu(i, c0, off, last=False):
                for q in range(2):
                    n = T_GU + 2 * (off + q)
                    act.wait_ge(pj_full, i * 4 + (n + 1))
                    if off or q:
                        act.wait_ge(pj_dve, i * 2 + taken(T_GU + 2 * (off + q) - 1, "D"))
                    act.activation(two(sg[:, :]), pj_view(n), ACT.Silu).then_inc(pj_act, 1)
                    for k in range(2):
                        c = c0 + 2 * q + k + 2
                        if last and q == 1:
                            continue
                        act.wait_ge(raw_in[c % 4], i * 16 + 16 * (c // 4 + 1))
                        if c - 2 >= C_GU:
                            wait_used(act, c - 2, i, 4)
                        act.activation(whi[:, ring(c) % 2, 0:1024], raw[:, c % 4, :], ACT.Copy).then_inc(w_hi, 1)
                    act.wait_ge(pj_dve, i * 2 + taken(n + 1, "D"))
                    act.activation(fh[:, bass.ds(i * 2 + (off + q), 1), :].rearrange("p a n -> p (a n)"),
                                   ft[:, :], ACT.Copy).then_inc(f_hi, 1)

            gu(0, C_GU, 0)
            with act.Fori(0, FC // 2 - 2) as i:
                gu(i, C_GU + 4, 2)
            gu(0, C_GU + 4 * (FC // 2 - 1), FC - 2, last=True)

            def hi_down(d, k):
                act.wait_ge(down_in[k], 16 * (d + 1))
                wait_used(act, C_DN + 2 * d + k - 2)
                act.activation(whi[:, (ring(C_DN) + k) % 2, :], rawd[:, k, :], ACT.Copy).then_inc(w_hi, 1)

            hi_down(0, 0)
            hi_down(0, 1)
            for d in range(KC):
                n = T_DN + d
                if d < KC - 1:
                    hi_down(d + 1, 0)
                    hi_down(d + 1, 1)
                act.wait_ge(pj_full, n + 1)
                act.activation(two(ymix[:, d, :]), pj_view(n), ACT.Copy).then_inc(pj_act, 1)
                act.wait_ge(acc_ready, KC + d)
                act.wait_ge(pj_act, taken(n, "A"))
                if d == 0:
                    act.wait_ge(f_lo, FC)
                act.activation(sq2[:, :], ymix[:, d, :], ACT.Square).then_inc(ysq_ready, 1)
            act.wait_ge(acc_ready, 2 * KC)
            n = tile_of["stat3"]
            act.wait_ge(pj_full, n + 1)
            act.activation(two(sq2[:, :]), pj_view(n), ACT.Sqrt, bias=eps[:, 0:1], scale=1.0 / D).then_inc(pj_act, 1)

        @block.gpsimd
        def _(pool):
            pool.memset(cstat[:, :, :].bitcast(F32), 0.0).then_inc(consts, 1)
            pool.memset(ones[:, :], 1.0).then_inc(consts, 1)
            pool.memset(eps[:, :], EPS).then_inc(consts, 1)

            def lo(c):
                sem_of_raw(pool, c)
                pool.wait_ge(w_hi, c + 1)
                name = CH[c] if c < C_OUT else None
                if name and name[0] == "v":
                    dst, h, src = wv_l[:, name[1], :], wv_h[:, name[1], :], raw[:, c % 4, 0:VWI]
                else:
                    slot_free(pool, c)
                    dst, h, src = (wlo[:, ring(c) % 2, 0:1024], whi[:, ring(c) % 2, 0:1024], raw[:, c % 4, :])
                pool.tensor_tensor(dst, src, h.bitcast(F32), ALU.subtract).then_inc(w_lo, 1)

            def xr(src, rstd, dst, n):
                pool.wait_ge(rstd_ready, {0: 1, 1: 3}[n])
                for kc in range(KC):
                    if kc >= 2:
                        pool.wait_ge(hf_ready, n * KC + kc - 1)
                    pool.tensor_tensor(dst[:, kc % 2, :], src[:, kc, :], rstd[:, :], ALU.mult).then_inc(xr_ready, 1)

            xr(xt, rstd0, xr0, 0)
            lo(N_ADA0)
            lo(N_ADA0 + 1)
            for s in SCHED:
                if s[0] == "end":
                    c = s[1]
                    r = ROPE_AT[CH[c]]
                    pool.wait_ge(pj_act, taken(tile_of[c], "A"))
                    if r >= 1:
                        pool.wait_ge(rope_o, r)
                    pool.tensor_tensor(zc[:, :], z[:, :], cos[:, :], ALU.mult).then_inc(zc_ready, 1)
                    nxt = c + 2
                    if nxt < C_V or (c >= C_V and nxt < C_OUT):
                        lo(nxt)
                elif s[0] == "vload":
                    for k in range(KC + 2):
                        lo(C_V + k)
                elif s[0] == "v" and s[2] == 1:
                    pool.wait_ge(pj_act, taken(tile_of[("v", 1)], "A"))
                    pool.dma_start(o["v_p"], vt[:, 3:7, 0:VW]).then_inc(vp_out, 16)
            c = AT[("ga", 0)]
            for d in range(KC):
                for q in range(7):
                    if c + 2 < C_OUT + 2:
                        lo(c + 2)
                        c += 1
                pool.wait_ge(m_hi, d + 1)
                pool.tensor_tensor(ml[:, d, :], mt[:, :], mh[:, d, :].bitcast(F32), ALU.subtract).then_inc(m_lo, 1)
            pool.wait_ge(ada_used, 48)
            pool.memset(acc1[:, :], 0.0).then_inc(acc_zero, 1)
            pool.wait_ge(acc_zero, 1)
            for d in range(KC):
                lo(C_OUT + d + 2)
                pool.wait_ge(ysq_ready, d + 1)
                if d:
                    pool.wait_ge(acc_ready, d)
                pool.tensor_tensor(acc1[:, :], acc1[:, :], sq1[:, d % 2, :], ALU.add).then_inc(acc_ready, 1)
            pool.wait_ge(xres_in, 16)
            for kc in range(0, KC, 2):
                pool.wait_ge(yg_ready, kc + 1)
                pool.tensor_tensor(x1[:, kc, :], ymix[:, kc, :], xres[:, kc, :], ALU.add).then_inc(x1_pool, 1)
            pool.wait_ge(x1_dve, KC // 2)
            pool.wait_ge(x1_pool, KC // 2)
            xr(x1, rstd2, xr1, 1)

            def gu_lo(i, c0, last=False):
                for q in range(2):
                    for k in range(2):
                        c = c0 + 2 * q + k + 2
                        if last and q == 1:
                            continue
                        pool.wait_ge(raw_in[c % 4], i * 16 + 16 * (c // 4 + 1))
                        pool.wait_ge(w_hi, i * 4 + (c + 1))
                        wait_used(pool, c - 2, i, 4)
                        s = ring(c) % 2
                        pool.tensor_tensor(wlo[:, s, 0:1024], raw[:, c % 4, :], whi[:, s, 0:1024].bitcast(F32),
                                           ALU.subtract).then_inc(w_lo, 1)

            with pool.Fori(0, FC // 2 - 1) as i:
                gu_lo(i, C_GU)
            gu_lo(0, C_GU + 4 * (FC // 2 - 1), last=True)
            pool.wait_ge(pj_full, tile_of["stat1"] + 1)
            pool.memset(acc2[:, :], 0.0).then_inc(acc_zero, 1)
            pool.wait_ge(acc_zero, 2)

            def lo_down(d, k):
                s = (ring(C_DN) + k) % 2
                pool.wait_ge(down_in[k], 16 * (d + 1))
                pool.wait_ge(w_hi, C_DN + 2 * d + k + 1)
                wait_used(pool, C_DN + 2 * d + k - 2)
                pool.tensor_tensor(wlo[:, s, :], rawd[:, k, :], whi[:, s, :].bitcast(F32), ALU.subtract)\
                    .then_inc(w_lo, 1)

            lo_down(0, 0)
            lo_down(0, 1)
            for d in range(KC):
                if d < KC - 1:
                    lo_down(d + 1, 0)
                    lo_down(d + 1, 1)
                pool.wait_ge(ysq_ready, KC + d + 1)
                pool.wait_ge(acc_ready, KC + d)
                pool.tensor_tensor(acc2[:, :], acc2[:, :], sq2[:, :], ALU.add).then_inc(acc_ready, 1)

        @block.vector
        def _(v):
            chain = [0]

            def link(ins):
                chain[0] += 1
                ins.then_inc(dve, 1)
                v.wait_ge(dve, chain[0])

            v.wait_ge(const_in, 16 * 9)
            v.wait_ge(consts, 3)
            v.wait_ge(c_hi, 1)
            v.tensor_tensor(cstat[:, :, 2:4], cf[:, :, :], cstat[:, :, 0:2].bitcast(F32), ALU.subtract)\
             .then_inc(c_lo, 1)
            link(v.tensor_tensor(lamv[:, 0:2, :], lamv[:, 0:2, :], lamv[:, 2:4, :], ALU.mult))
            v.tensor_reduce(lam[:, 0:2], lamv[:, 0:2, :], AX.X, ALU.add).then_inc(lam_dots, 1)

            def ada_columns(n):
                v.wait_ge(ada_cols, n + 1)
                link(v.tensor_copy(t4[:, :, :], pvb[:, 0:16].rearrange("p (a b) -> p a b", a=4)))
                dst = ada[:, 4 * n:4 * n + 4, :]
                link(v.tensor_tensor(dst, t4[:, :, 0:2], t4[:, :, 2:4], ALU.add))
                v.tensor_tensor(dst, dst, bada[:, 4 * n:4 * n + 4, :], ALU.add).then_inc(ada_done, 1)

            def lo(c):
                sem_of_raw(v, c)
                v.wait_ge(w_hi, c + 1)
                s = ring(c) % 2
                v.tensor_tensor(wlo[:, s, 0:1024], raw[:, c % 4, :], whi[:, s, 0:1024].bitcast(F32), ALU.subtract)\
                 .then_inc(w_lo_dve, 1)

            lo(0)
            lo(1)
            for c in range(N_ADA0):
                if c + 2 < N_ADA0:
                    lo(c + 2)
                if c % 4 == 3 and c > 3:
                    ada_columns(c // 4 - 1)
                if c == 12:
                    v.wait_ge(pj_act, 1)
                    v.reciprocal(rstd0[:, :], rms0[:, :]).then_inc(rstd_ready, 1)
            ada_columns(3)
            v.wait_ge(ada_done, 4)

            def gain_scale(n, sc):
                for w in range(2):
                    v.scalar_tensor_tensor(out=gs[:, n, :, w], in0=ada[:, sc:sc + KC, w], scalar=1.0,
                                           in1=gains[:, 2 * n, :], op0=ALU.add, op1=ALU.mult).then_inc(dve, 1)
                    chain[0] += 1
                v.wait_ge(dve, chain[0])

            gain_scale(0, KC)
            SPANS = ((1, 0, NS), (0, NS, T))

            def modulate(n, sh, xr, hf, hi_, lo_):
                for kc in range(KC):
                    v.wait_ge(xr_ready, n * KC + kc + 1)
                    if kc >= 2:
                        v.wait_ge(h_lo, n * KC + kc - 1)
                    for w, c0, c1 in SPANS:
                        ins = v.tensor_scalar(hf[:, kc % 2, c0:c1], xr[:, kc % 2, c0:c1], gs[:, n, kc, w:w + 1],
                                              ada[:, sh + kc, w:w + 1], ALU.mult, ALU.add)
                    ins.then_inc(hf_ready, 1)
                    v.wait_ge(h_hi, n * KC + kc + 1)
                    v.tensor_tensor(lo_[:, kc, :], hf[:, kc % 2, :], hi_[:, kc, :].bitcast(F32), ALU.subtract)\
                     .then_inc(h_lo, 1)

            modulate(0, 0, xr0, hf0, hh, hl)
            v.wait_ge(lam_exp, 1)
            link(v.tensor_tensor(lam[:, 2:3], lam[:, 0:1], lam[:, 1:2], ALU.subtract))
            link(v.tensor_scalar(lam[:, 2:3], lam[:, 2:3], -1.0, -LAM_INIT, ALU.mult, ALU.add))
            t1 = mb[:, MBOFF[1]:MBOFF[1] + NKEY[1]]
            link(v.memset(t1, 0.0))
            link(v.memset(mb[0:64, MBOFF[1] + 64:MBOFF[1] + P], NEG))

            def rope(c):
                name = CH[c]
                r = ROPE_AT[name]
                v.wait_ge(pj_act, taken(tile_of[c], "A"))
                v.tensor_tensor(zs[64:128, :], z[0:64, :], sin[0:64, :], ALU.mult).then_inc(dve, 1)
                v.tensor_tensor(zs[0:64, :], z[64:128, :], sin[64:128, :], ALU.mult).then_inc(dve, 1)
                chain[0] += 2
                v.wait_ge(dve, chain[0])
                v.wait_ge(zc_ready, r + 1)
                if r >= 2:
                    v.wait_ge(rope_hi, r - 1)
                    v.wait_ge(rope_lo, r - 1)
                    if ROPES[r - 2] in KT_AT:
                        v.wait_ge(k_out[KT_AT[ROPES[r - 2]]], 16)
                v.tensor_tensor(ro[:, r % 2, PAST:KEYS], zc[:, :], zs[:, :], ALU.add).then_inc(rope_o, 1)
                v.wait_ge(rope_hi, r + 1)
                if name in KT_AT:
                    dst = kz_of(name)
                    for m in range(2):
                        ins = v.scalar_tensor_tensor(out=dst[:, 1, m, :], in0=ro[:, r % 2, :], scalar=hmask[:, m:m + 1],
                                                     in1=dst[:, 0, m, :].bitcast(F32), op0=ALU.mult, op1=ALU.subtract)
                    ins.then_inc(rope_lo, 1)
                else:
                    qh, ql = q_of(name)
                    v.tensor_tensor(ql, ro[:, r % 2, PAST:KEYS], qh.bitcast(F32), ALU.subtract).then_inc(rope_lo, 1)

            ix = 0
            for s in SCHED:
                if s[0] == "end":
                    rope(s[1])
                elif s[0] == "v":
                    t = s[2]
                    v.wait_ge(pj_act, taken(tile_of[("v", t)], "A"))
                    link(v.tensor_scalar(wis[:, t, :], vt[:, 2 if t == 0 else 2 + t, VW:VWI], IDX_SCALE, None, ALU.mult))
                elif s[0] == "idx":
                    t, h = s[1], s[2]
                    m = mb[:, MBOFF[t]:MBOFF[t] + NKEY[t]]
                    r = ee[:, 0, ix % 2, 0:NKEY[t]]
                    v.wait_ge(ix_relu, ix + 1)
                    if h == 0:
                        v.tensor_scalar(m, r, wis[:, t, 0:1], None, ALU.mult).then_inc(ix_acc, 1)
                    else:
                        v.wait_ge(ix_acc, ix)
                        v.scalar_tensor_tensor(out=m, in0=r, scalar=wis[:, t, h:h + 1], in1=m, op0=ALU.mult,
                                               op1=ALU.add).then_inc(ix_acc, 1)
                    ix += 1
                elif s[0] == "idxmask":
                    t = s[1]
                    v.wait_ge(ix_acc, ix)
                    if t:
                        link(v.memset(mb[0:64, MBOFF[t] + NKEY[t] - 64:MBOFF[t] + NKEY[t]], OUT_OF_REACH))
                elif s[0] == "topk":
                    t, r = s[1], s[2]
                    m = mb[:, MBOFF[t]:MBOFF[t] + NKEY[t]]
                    link(v.max(top8[:, :], m))
                    link(v.match_replace(out=m, in_to_replace=top8[:, :], in_values=m, imm_value=TAKEN))
                    if r == ROUNDS[t] - 1:
                        link(v.tensor_scalar(m, m, (OUT_OF_REACH + TAKEN) / 2, NEG, ALU.is_gt, ALU.mult))
                elif s[0] == "qk":
                    u = s[1]
                    g, t, diff = unit(u)
                    n = NKEY[t]
                    v.wait_ge(qk_ready, u + 1)
                    if diff:
                        if t:
                            link(v.memset(lg[0:64, :, n - 64:n], NEG))
                        link(v.tensor_reduce(mx[:, u, :], lg[:, :, 0:n], AX.X, ALU.max))
                    else:
                        v.wait_ge(tr_ready, transposes_before(u - 1))
                        m_ = mb[:, MBOFF[t]:MBOFF[t] + n]
                        for m in range(2):
                            ins = v.tensor_tensor_reduce(out=ee[:, u % 2, m, 0:n], in0=lg[:, m, 0:n], in1=m_, scale=1.0,
                                                         scalar=NEG, op0=ALU.add, op1=ALU.max,
                                                         accum_out=mx[:, u, m:m + 1])
                            link(ins)
                    v.tensor_scalar(nmx[:, u, :], mx[:, u, :], -SCALE, None, ALU.mult).then_inc(mx_ready, 1)
                elif s[0] == "comb":
                    u = s[1]
                    g, t, diff = unit(u)
                    n = NKEY[t]
                    v.wait_ge(e_ready, u + 1)
                    link(v.reciprocal(rsum[:, u, :], esum[:, u, :]))
                    e0, e1_ = ee[:, u % 2, 0, 0:n], ee[:, u % 2, 1, 0:n]
                    if diff:
                        link(v.tensor_scalar(nlr[:, u:u + 1], rsum[:, u, 1:2], lam[:, 2:3], None, ALU.mult))
                        link(v.tensor_scalar(e1_, e1_, nlr[:, u:u + 1], None, ALU.mult))
                        ins = v.scalar_tensor_tensor(out=e0, in0=e0, scalar=rsum[:, u, 0:1], in1=e1_, op0=ALU.mult,
                                                     op1=ALU.add)
                        if t == 0:
                            link(ins)
                    if t == 0:
                        for m in range(1 if diff else 2):
                            ins = v.memset(ee[:, u % 2, m, n:NBLK[0] * P], 0.0)
                    if diff or t == 0:
                        ins.then_inc(p_ready, 1)
                elif s[0] == "pv":
                    u = s[1]
                    g, t, diff = unit(u)
                    v.wait_ge(pv_ready, u + 1)
                    if diff:
                        if u == 0:
                            v.wait_ge(ix_full, 32)
                        link(v.tensor_copy(ob[:, u, :], pvb[:, 0:P]))
                        v.tensor_tensor_reduce(out=on[:, :], in0=ob[:, u, :], in1=ob[:, u, :], scale=1.0, scalar=0.0,
                                               op0=ALU.mult, op1=ALU.add, accum_out=osq[:, u:u + 1]).then_inc(o_ready, 1)
                        v.wait_ge(o_ready, u + 1)
                    else:
                        if u > 20:
                            v.wait_ge(oT_full, u - 20)
                        for m in range(2):
                            ins = v.tensor_scalar(on[:, m * HD:m * HD + HD], pvb[:, m * P + m * HD:m * P + m * HD + HD],
                                                  rsum[:, u, m:m + 1], None, ALU.mult)
                        ins.then_inc(o_ready, 1)
                        v.wait_ge(oT_full, u - 20 + 1)
                        v.tensor_copy(oT[:, g - 4, QCOL[t]:QCOL[t] + QUSE[t]], pvb[:, 256:256 + QUSE[t]]).then_inc(oT_done, 1)
                elif s[0] == "bnorm":
                    v.wait_ge(on_rms, 1)
                    link(v.reciprocal(orms[:, :], orms[:, :]))
                    for t in range(5):
                        for h in range(4):
                            ins = v.tensor_scalar(ob[:, 5 * h + t, :], ob[:, 5 * h + t, :],
                                                  orms[:, 5 * h + t:5 * h + t + 1], 1.0 - LAM_INIT, ALU.mult, ALU.mult)
                        ins.then_inc(on_ready, 1)
                    for t in range(5):
                        v.wait_ge(ob_full, t + 1)
                        v.tensor_copy(oT[:, 4:8, QCOL[t]:QCOL[t] + QUSE[t]],
                                      pvb[:, :].rearrange("p (h q) -> p h q", h=4)[:, :, 0:QUSE[t]]).then_inc(ob_done, 1)
            for kc in range(KC):
                v.wait_ge(ot_hi, kc + 1)
                v.tensor_tensor(otl[:, kc, :], oT[:, kc, :], oth[:, kc, :].bitcast(F32), ALU.subtract).then_inc(ot_lo, 1)
            for d in range(KC):
                n = tile_of[("oa", d)]
                v.wait_ge(pj_full, n + 1)
                v.wait_ge(pj_act, taken(tile_of[("gb", d)], "A"))
                v.tensor_tensor(two(sga[:, :]), pj_view(n), two(sga[:, :]), ALU.mult).then_inc(pj_dve, 1)
                v.wait_ge(pj_full, n + 2)
                v.tensor_tensor(two(sgb[:, :]), pj_view(n + 1), two(sgb[:, :]), ALU.mult).then_inc(pj_dve, 1)
                v.wait_ge(pj_dve, taken(n + 1, "D"))
                if d:
                    v.wait_ge(m_hi, d)
                    v.wait_ge(m_lo, d)
                v.tensor_tensor(mt[:, :], sga[:, :], sgb[:, :], ALU.add).then_inc(m_ready, 1)
                ada_columns(4 + d)
            v.wait_ge(ada_done, 12)
            gain_scale(1, 4 * KC)
            for n, gt in ((0, 2), (1, 5)):
                for w in range(2):
                    link(v.tensor_tensor(gg[:, n, :, w], ada[:, gt * KC:gt * KC + KC, w], gains[:, 2 * n + 1, :], ALU.mult))

            def gated(n, rstd, kc):
                for w, c0, c1 in SPANS:
                    ins = v.scalar_tensor_tensor(out=ymix[:, kc, c0:c1], in0=ymix[:, kc, c0:c1],
                                                 scalar=gg[:, n, kc, w:w + 1], in1=rstd[:, c0:c1], op0=ALU.mult,
                                                 op1=ALU.mult)
                ins.then_inc(yg_ready, 1)

            v.wait_ge(pj_act, taken(tile_of["stat1"], "A"))
            v.reciprocal(rstd1[:, :], rms1[:, :]).then_inc(rstd_ready, 1)
            v.wait_ge(rstd_ready, 2)
            v.wait_ge(xres_in, 16)
            for kc in range(KC):
                gated(0, rstd1, kc)
                if kc % 2:
                    v.wait_ge(yg_ready, kc + 1)
                    v.tensor_tensor(x1[:, kc, :], ymix[:, kc, :], xres[:, kc, :], ALU.add).then_inc(x1_dve, 1)
            v.wait_ge(pj_act, taken(tile_of["stat2"], "A"))
            v.reciprocal(rstd2[:, :], rms1[:, :]).then_inc(rstd_ready, 1)
            v.wait_ge(x1_dve, KC // 2)
            v.wait_ge(x1_pool, KC // 2)
            modulate(1, 3 * KC, xr1, hf1, hh2, hl2)

            def ffn(i, off):
                for q in range(2):
                    n = T_GU + 2 * (off + q)
                    v.wait_ge(pj_full, i * 4 + (n + 2))
                    v.wait_ge(pj_act, i * 2 + taken(n, "A"))
                    if off or q:
                        v.wait_ge(f_lo, i * 2 + (off + q))
                    v.tensor_tensor(two(ft[:, :]), pj_view(n + 1), two(sg[:, :]), ALU.mult).then_inc(pj_dve, 1)
                    v.wait_ge(pj_dve, i * 2 + taken(n + 1, "D"))
                    v.wait_ge(f_hi, i * 2 + (off + q + 1))
                    at_ = bass.ds(i * 2 + (off + q), 1)
                    v.tensor_tensor(fl[:, at_, :].rearrange("p a n -> p (a n)"), ft[:, :],
                                    fh[:, at_, :].rearrange("p a n -> p (a n)").bitcast(F32), ALU.subtract).then_inc(f_lo, 1)

            ffn(0, 0)
            with v.Fori(0, FC // 2 - 1) as i:
                ffn(i, 2)
            v.wait_ge(pj_act, taken(tile_of["stat3"], "A"))
            v.reciprocal(rstd3[:, :], sq2[:, :]).then_inc(rstd_ready, 1)
            v.wait_ge(rstd_ready, 4)
            for kc in range(KC):
                gated(1, rstd3, kc)
                v.wait_ge(yg_ready, KC + kc + 1)
                v.tensor_tensor(x1[:, kc, :], ymix[:, kc, :], x1[:, kc, :], ALU.add).then_inc(y_fin, 1)

        @block.tensor
        def _(pe):
            mm = pe.matmul
            pe.wait_ge(const_in, 16 * 9)
            pe.wait_ge(consts, 2)
            pe.wait_ge(c_lo, 1)

            def ada_chunk(c, n, q):
                wait_lo(pe, c)
                s = ring(c) % 2
                if q == 0 and n:
                    pe.wait_ge(ada_sb, n)
                for k in range(2):
                    kc = 2 * q + k
                    for w, part in ((whi, 0), (wlo, 1)):
                        ins = mm(tb[:, :], cstat[:, kc, :], w[:, s, k * 512:(k + 1) * 512],
                                 start=(kc == 0 and part == 0), stop=(kc == KC - 1 and part == 1))
                ins.then_inc(ada_used, 1)

            def ada_rows_done(n, c, rows_):
                pe.wait_ge(ada_sb, n + 1)
                if n:
                    pe.wait_ge(ada_done, n)
                for k in range(4):
                    ins = pe.transpose(pvb[:, 4 * k:4 * k + 4], rows_[0:4, k * P:(k + 1) * P], ident[0:4, 0:4])
                ins.then_inc(ada_cols, 1)

            def stat(tile, src, first, n=KC):
                pj_free(pe, tile)
                for kc in range(n):
                    pe.wait_ge(sq_ready, first + kc + 1)
                    for h in range(2):
                        x = src(kc)[:, h * HALF:(h + 1) * HALF]
                        ins = mm(pj[tile % 2][:, h, 0:HALF], ones[:, :], x, start=(kc == 0), stop=(kc == n - 1))
                    ins.then_inc(sq_used if kc < n - 1 else pj_full, 1)

            def blocks(c, slot, tile, kcs, xh, xl, first, last, off=0):
                for kc in kcs:
                    b = (kc + off) * P
                    for w, x in ((whi, xh), (whi, xl), (wlo, xh)):
                        for h in range(2):
                            ins = mm(pj[tile % 2][:, h, 0:HALF], w[:, slot, b:b + P], x[:, kc if off == 0 else kc, h * HALF:(h + 1) * HALF],
                                     start=(kc == first and w is whi and x is xh),
                                     stop=(kc == last and w is wlo))
                return ins

            stat(tile_of["stat0"], lambda kc: sq0[:, kc % 2, :], 0)
            for c in range(N_ADA0):
                n, q = divmod(c, 4)
                ada_chunk(c, n, q)
                if q == 3:
                    ada_rows_done(n, c, rowa)

            ix = 0
            sets = 0
            pe.wait_ge(h_lo, 1)
            for s in SCHED:
                if s[0] == "part":
                    c, k0, k1 = s[1], s[2], s[3]
                    if k0 == 0:
                        wait_lo(pe, c)
                        pj_free(pe, tile_of[c])
                    for kc in range(k0, k1):
                        if c == N_ADA0:
                            pe.wait_ge(h_lo, kc + 1)
                        ins = blocks(c, ring(c) % 2, tile_of[c], [kc], hh, hl, 0, KC - 1)
                elif s[0] == "end":
                    ins.then_inc(pj_full, 1)
                elif s[0] == "vload":
                    wait_lo(pe, C_V + KC - 1)
                elif s[0] == "v":
                    t = s[2]
                    tile = tile_of[("v", t)]
                    pj_free(pe, tile)
                    q = slice(QCOL[t], QCOL[t] + P)
                    for kc in range(KC):
                        for x, w in ((hh, wv_h), (hh, wv_l), (hl, wv_h)):
                            for h in range(2):
                                ins = mm(pj[tile % 2][:, h, 0:VH], x[:, kc, q], w[:, kc, h * VH:(h + 1) * VH],
                                         start=(kc == 0 and w is wv_h and x is hh), stop=(kc == KC - 1 and x is hl))
                    ins.then_inc(pj_full, 1)
                elif s[0] == "idx":
                    t, h = s[1], s[2]
                    if ix == 0:
                        pe.wait_ge(rope_lo, N_KI)
                    if ix >= 2:
                        pe.wait_ge(ix_relu, ix - 1)
                    j, m = divmod(h, 2)
                    logits(pe, lg[:, ix % 2, 0:NMOV[t]], qi_h[:, j, :], qi_l[:, j, :], ki, m, t).then_inc(ix_full, 1)
                    ix += 1
                elif s[0] == "qk":
                    u = s[1]
                    g, t, diff = unit(u)
                    if u == 0:
                        pe.wait_ge(ix_relu, 32)
                    elif unit(u - 1)[2]:
                        pe.wait_ge(e_ready, u)
                    else:
                        pe.wait_ge(mx_ready, u)
                    pe.wait_ge(rope_lo, last_rope(g) + 1)
                    qt = q1 if g % 2 else q0
                    kt = (kz1 if g % 2 else kz0) if diff else kz0
                    for m in range(2):
                        ins = logits(pe, lg[:, m, 0:NMOV[t]], qt[:, 0, :], qt[:, 1, :], kt, m, t)
                    ins.then_inc(qk_ready, 1)
                elif s[0] == "tr":
                    u = s[1]
                    g, t, diff = unit(u)
                    if diff or t == 0:
                        pe.wait_ge(p_ready, u + 1 if diff else 21 + (u - 20) // 5)
                    else:
                        pe.wait_ge(e_ready, u + 1)
                    for m in range(1 if diff else 2):
                        if sets:
                            pe.wait_ge(pt_ready, sets)
                        for b in range(NBLK[t]):
                            ins = pe.transpose(tb[:, b * P:(b + 1) * P], ee[:, u % 2, m, b * P:(b + 1) * P], ident[:, :])
                        ins.then_inc(tr_ready, 1)
                        sets += 1
                elif s[0] == "pv":
                    u = s[1]
                    g, t, diff = unit(u)
                    if u and u <= 20:
                        pe.wait_ge(o_ready, u)
                    if u == 0:
                        pe.wait_ge(const_in, 16 * 10)
                    if u == 20:
                        pe.wait_ge(ob_done, 5)
                    if u > 20:
                        pe.wait_ge(oT_done, u - 20)
                    first_set = sets - (1 if diff else 2)
                    for m in range(1 if diff else 2):
                        pe.wait_ge(pt_ready, first_set + m + 1)
                        col = AKV + P * g if diff else 0
                        for b in range(NBLK[t]):
                            ins = mm(pvb[:, m * P:(m + 1) * P], pt[:, (first_set + m) % 2, b * P:(b + 1) * P],
                                     vt[:, VBLK[t] + b, col:col + P], start=(b == 0), stop=(b == NBLK[t] - 1))
                        ins.then_inc(pt_used if not diff and m == 0 else pv_ready, 1)
                    if not diff:
                        pe.wait_ge(o_ready, u + 1)
                        pe.transpose(pvb[:, 256:256 + P], on[:, :], ident[:, :]).then_inc(oT_full, 1)
                elif s[0] == "bnorm":
                    for t in range(5):
                        pe.wait_ge(on_ready, t + 1)
                        if t:
                            pe.wait_ge(ob_done, t)
                        for h in range(4):
                            ins = pe.transpose(pvb[:, h * P:(h + 1) * P], ob[:, 5 * h + t, :], ident[:, :])
                        ins.then_inc(ob_full, 1)
            c = AT[("ga", 0)]
            for d in range(KC):
                for name in ("ga", "gb"):
                    tile = tile_of[(name, d)]
                    wait_lo(pe, c)
                    pj_free(pe, tile)
                    blocks(c, ring(c) % 2, tile, range(KC), hh, hl, 0, KC - 1).then_inc(pj_full, 1)
                    c += 1
                for q in range(4):
                    if d == 0 and q == 0:
                        pe.wait_ge(pt_ready, sets)
                    ada_chunk(c, 4 + d, q)
                    c += 1
                wait_lo(pe, c)
                if d == 0:
                    pe.wait_ge(ot_lo, KC)
                for i, name in enumerate(("oa", "ob")):
                    tile = tile_of[(name, d)]
                    pj_free(pe, tile)
                    ins = blocks(c, ring(c) % 2, tile, range(4 * i, 4 * i + 4), oth, otl, 4 * i, 4 * i + 3)
                    ins.then_inc(pj_full, 1)
                c += 1
                ada_rows_done(4 + d, c, rowb)
            for d in range(KC):
                tile = T_OUT + d
                wait_lo(pe, c)
                pe.wait_ge(m_lo, KC)
                pj_free(pe, tile)
                blocks(c, ring(c) % 2, tile, range(KC), mh, ml, 0, KC - 1).then_inc(pj_full, 1)
                c += 1
            pe.wait_ge(acc_ready, KC)
            tile = tile_of["stat1"]
            pj_free(pe, tile)
            for h in range(2):
                ins = mm(pj[tile % 2][:, h, 0:HALF], ones[:, :], acc1[:, h * HALF:(h + 1) * HALF], start=True, stop=True)
            ins.then_inc(pj_full, 1)
            stat(tile_of["stat2"], lambda kc: sq1[:, kc % 2, :], KC)

            def gu(i, off):
                for q in range(4):
                    tile = T_GU + 2 * off + q
                    cc = C_GU + 2 * off + q
                    pe.wait_ge(w_lo, i * 4 + lo_count(cc))
                    who = takers[tile - 2]
                    if tile - 2 >= T_GU:
                        pe.wait_ge(pj_act if who == "A" else pj_dve, i * 2 + taken(tile - 2, who))
                    else:
                        pj_free(pe, tile)
                    for kc in range(KC):
                        if off == 0 and q == 0:
                            pe.wait_ge(h_lo, KC + kc + 1)
                        ins = blocks(cc, ring(cc) % 2, tile, [kc], hh2, hl2, 0, KC - 1)
                    ins.then_inc(pj_full, 1)

            gu(0, 0)
            with pe.Fori(0, FC // 2 - 1) as i:
                gu(i, 2)
            for d in range(KC):
                tile = T_DN + d
                pj_free(pe, tile)
                for k in range(2):
                    cc = C_DN + 2 * d + k
                    pe.wait_ge(w_lo, lo_count(cc))
                    if d == 0:
                        pe.wait_ge(f_lo, FC)
                    s = (ring(C_DN) + k) % 2
                    for b in range(BLK_DOWN):
                        kc = BLK_DOWN * k + b
                        for w, x in ((whi, fh), (whi, fl), (wlo, fh)):
                            for h in range(2):
                                ins = mm(pj[tile % 2][:, h, 0:HALF], w[:, s, b * P:(b + 1) * P],
                                         x[:, kc, h * HALF:(h + 1) * HALF],
                                         start=(kc == 0 and w is whi and x is fh), stop=(kc == FC - 1 and w is wlo))
                    ins.then_inc(pj_full if k else down_used, 1)
            pe.wait_ge(acc_ready, 2 * KC)
            tile = tile_of["stat3"]
            pj_free(pe, tile)
            for h in range(2):
                ins = mm(pj[tile % 2][:, h, 0:HALF], ones[:, :], acc2[:, h * HALF:(h + 1) * HALF], start=True, stop=True)
            ins.then_inc(pj_full, 1)


def logits(pe, dst, qh, ql, kt, m, t):
    n = NMOV[t]
    q, k = slice(QCOL[t], QCOL[t] + P), slice(KCOL[t], KCOL[t] + n)
    pe.matmul(dst, qh[:, q], kt[:, 0, m, k], start=True, stop=False)
    pe.matmul(dst, ql[:, q], kt[:, 0, m, k], start=False, stop=False)
    return pe.matmul(dst, qh[:, q], kt[:, 1, m, k], start=False, stop=True)


def pair(a, b):
    h = HD // 2
    return [*range(a, a + h), *range(b, b + h), *range(a + h, a + HD), *range(b + h, b + HD)]


C_QA, C_KA, C_VA, C_QI = 0, AW, AW + AKV, AW + 2 * AKV
C_KI = C_QI + IQ
C_WI = C_KI + HD
C_QB = C_WI + IH
C_KB, C_VB = C_QB + BW, C_QB + 2 * BW
C_GA = C_VB + BW
C_GB = C_GA + D

IN_CHUNKS = ([(("ki", 0), pair(C_KI, C_KI))]
             + [(("qi", j), pair(C_QI + 2 * j * HD, C_QI + (2 * j + 1) * HD)) for j in range(4)]
             + [((n, h), pair(b + P * h, b + P * h + HD)) for h in range(4) for n, b in (("kb", C_KB), ("qb", C_QB))]
             + [(("ka", 0), pair(C_KA, C_KA + HD))]
             + [(("qa", j), pair(C_QA + j * HD, C_QA + (j + 4) * HD)) for j in range(4)]
             + [((n, d), list(range(b + P * d, b + P * (d + 1)))) for d in range(KC) for n, b in (("ga", C_GA), ("gb", C_GB))])
W_ROW = {name: i for i, (name, _) in enumerate(IN_CHUNKS)}
S_WO = len(IN_CHUNKS)
W_ROW.update({("wo", d): S_WO + d for d in range(KC)})
S_OUT = S_WO + KC


def kernel(**inputs):
    import numpy as _np
    import concourse.bacc as _bacc
    from concourse import mybir as _mybir
    from concourse.bass_utils import run_bass_kernel_spmd as _run

    x = {k: _np.asarray(v) for k, v in inputs.items()}

    def chunk(w):
        return w.reshape(-1, P, w.shape[1]).transpose(1, 0, 2).reshape(P, -1)

    def columns(v):
        return v.reshape(-1, P).T

    w_in = x["w_in"][0]
    ws = [chunk(w_in[:, cols]) for _, cols in IN_CHUNKS]
    rows_a = [r for j in range(4) for b in (j, j + 4) for r in range(b * HD, (b + 1) * HD)]
    w_o = _np.concatenate([x["w_o_a"][0][rows_a], x["w_o_b"][0]], axis=0)
    ws += [chunk(w_o[:, d * P:(d + 1) * P]) for d in range(KC)]
    ws += [chunk(x["w_out"][0][:, d * P:(d + 1) * P]) for d in range(KC)]
    for i in range(FC):
        ws += [chunk(x[n][0][:, i * P:(i + 1) * P]) for n in ("w_gate", "w_up")]
    v_cols = [*range(C_VA, C_VA + AKV), *range(C_VB, C_VB + BW), *range(C_WI, C_WI + IH)]
    w_d = _np.stack([chunk(x["w_down"][0][k * BLK_DOWN * P:(k + 1) * BLK_DOWN * P, d * P:(d + 1) * P])
                     for d in range(KC) for k in range(2)])
    w_ada = _np.stack([chunk(x["w_ada"][0][q * 256:(q + 1) * 256, n * 512:(n + 1) * 512])
                       for n in range(12) for q in range(4)])
    tokens = _np.concatenate([x["x_sample"][0], x["x_prompt"][0]], axis=0)
    pos = _np.concatenate([PAST + _np.arange(NS), _np.arange(NP_)]).astype(_np.float32)
    half = HD // 2
    inv = (1.0 / (_np.float32(10000.0) ** (_np.arange(half, dtype=_np.float32) / _np.float32(half)))).astype(_np.float32)
    ang = (pos[None, :] * inv[:, None]).astype(_np.float32)
    cos, sin = _np.cos(ang).astype(_np.float32), _np.sin(ang).astype(_np.float32)
    own = (_np.arange(P) // half) % 2
    ck = {"ki": [x["cache_idx_k"][0, 0]] * 2, "ka": [x["cache_a_k"][0, 0, :, j] for j in range(2)]}
    caches = []
    for name, j in KTILES:
        a_, b_ = ck[name] if name in ck else [x["cache_b_k"][0, 0, :, j, m] for m in range(2)]
        both = _np.concatenate([a_, b_], axis=1).T
        caches.append(both[pair(0, HD)])
    cv = _np.concatenate([x["cache_a_v"][0, 0].reshape(PAST, AKV), x["cache_b_v"][0, 0].reshape(PAST, BW)], axis=1)
    arrays = {
        "w_s": _np.stack(ws), "w_v": w_in[:, v_cols].reshape(KC, P, VWI), "w_ada": w_ada, "w_d": w_d,
        "xT": tokens.T.reshape(KC, P, T).transpose(1, 0, 2),
        "cT": _np.stack([columns(x["c_prompt"][0]), columns(x["c_sample"][0])], axis=2),
        "bada": _np.stack([columns(x["b_ada"][0])] * 2, axis=2),
        "gains": _np.stack([columns(x[n][0]) for n in ("g_pre_mix", "g_post_mix", "g_pre_ffn", "g_post_ffn")], axis=1),
        "lamv": _np.broadcast_to(_np.stack([x[n][0] for n in ("lam_q1", "lam_q2", "lam_k1", "lam_k2")])[None], (P, 4, HD)),
        "hmask": _np.stack([own == 0, own == 1], axis=1).astype(_np.float32),
        "cos": _np.tile(cos, (4, 1)), "sin": _np.concatenate([sin, sin, -sin, -sin], axis=0),
        "ident": _np.eye(P, dtype=_np.float32),
        "cache_k": _np.stack(caches), "cache_v": cv.reshape(2, P, VW).transpose(1, 0, 2),
    }
    arrays = {k: _np.ascontiguousarray(v) for k, v in arrays.items()}
    nc = _bacc.Bacc("TRN2", target_bir_lowering=False, num_devices=1)
    a = {k: nc.dram_tensor("in_" + k, v.shape, _mybir.dt.from_np(v.dtype), kind="ExternalInput").ap()
         for k, v in arrays.items()}
    outs = {"yT": (KC, P, T), "kT": (len(KTILES), P, T), "v_p": (P, 4, VW), "v_s": (NS, VW)}
    o = {k: nc.dram_tensor("out_" + k, s, F32, kind="ExternalOutput").ap() for k, s in outs.items()}
    build(nc, a, o)
    r = _run(nc, [{"in_" + k: v for k, v in arrays.items()}], core_ids=[0]).results[0]

    y = r["out_yT"].reshape(D, T).T
    back = _np.argsort(pair(0, HD))
    k = r["out_kT"][:, back].transpose(0, 2, 1)
    vp = r["out_v_p"].transpose(1, 0, 2).reshape(NP_, VW)
    vs = r["out_v_s"]
    kb = _np.stack([k[KT_AT[("kb", h)]] for h in range(4)], axis=1)
    res = [y[NS:].reshape(1, NP_, D), y[:NS].reshape(1, NS, D)]
    for rows, v in ((slice(NS, T), vp), (slice(0, NS), vs)):
        n = v.shape[0]
        res += [k[KT_AT[("ka", 0)]][rows].reshape(1, 1, n, 2, HD), v[:, :AKV].reshape(1, 1, n, 2, HD),
                k[0][rows][:, :HD].reshape(1, 1, n, HD), kb[rows].reshape(1, 1, n, 4, 2, HD),
                v[:, AKV:].reshape(1, 1, n, 4, 2 * HD)]
    return tuple(_np.ascontiguousarray(t) for t in res)
```

```python
import math
from contextlib import ExitStack

import numpy as np
import concourse.bass as bass
from concourse import mybir

F32 = mybir.dt.float32
F32R = mybir.dt.float32r
ALU = mybir.AluOpType
ACT = mybir.ActivationFunctionType
AX = mybir.AxisListType

P = 128
D = 1024
KC = D // P
NS, NP_ = 64, 512
T = NS + NP_
HALF = T // 2
PAST = 256
KEYS = PAST + T
HD = 64
FF = 2816
FC = FF // P
AW, AKV, IQ, IH = 512, 128, 512, 8
BW = 512
TOPK_P, TOPK_S = min(256, NP_ // 4), min(256, (PAST + NS) // 4)
VW = AKV + BW
VWI = VW + IH
VH = VWI // 2
EPS = 1e-6
SCALE = HD ** -0.5
IDX_SCALE = (IH * HD) ** -0.5
LAM_INIT = 0.8 - 0.6 * math.exp(-0.3 * 0)
OUT_OF_REACH = -2e38
TAKEN = -3e38
NEG = -1e30
BLK_DOWN = FC // 2

QCOL = [0] + [NS + P * i for i in range(4)]
KCOL = [0] + [PAST + NS] * 4
NKEY = [PAST + NS, P, 2 * P, 3 * P, 4 * P]
NMOV = [max(n, 256) for n in NKEY]
NBLK = [-(-n // P) for n in NKEY]
VBLK = [0, 3, 3, 3, 3]
QUSE = [NS, P, P, P, P]
ROUNDS = [TOPK_S // 8, 0] + [TOPK_P // 8] * 3
MBOFF = [sum(NKEY[:i]) for i in range(5)]
NG = 8
NU = NG * 5


RING, RAW, RAW0 = 3, 3, 7
N_ADA0 = 16


def group_chunks(g):
    return {0: [("kb", 1), ("qb", 1)], 1: [("kb", 2), ("qb", 2)], 2: [("kb", 3), ("qb", 3)],
            3: [("ka", 0), ("qa", 0)], 4: [("qa", 1)], 5: [("qa", 2)], 6: [("qa", 3)], 7: [("ga", 0)]}[g]


def plan():
    ch = [("ada", n, q) for n in range(4) for q in range(4)]
    ch += [("ki", 0)]
    for j in range(4):
        ch += [("v", 2 * j), ("v", 2 * j + 1), ("qi", j)]
    ch += [("kb", 0), ("qb", 0)]
    for g in range(NG):
        ch += group_chunks(g) + [("ada", 4 + g, q) for q in range(4)]
    ch += [("gb", 0)]
    for d in range(KC):
        ch += ([("ga", d + 1), ("gb", d + 1)] if d + 1 < KC else []) + [("wo", d)]
    return ch


CH = plan()
C_OUT = len(CH)
C_GU = C_OUT + KC
C_DN = C_GU + 2 * FC
AT = {c: i for i, c in enumerate(CH)}
IN_RING = [i for i, c in enumerate(CH) if c[0] != "v"]
RING_AT = {c: i for i, c in enumerate(IN_RING)}
ROPES = [c for c in CH if c[0] in ("ki", "qi", "kb", "qb", "ka", "qa")]
ROPE_AT = {c: i for i, c in enumerate(ROPES)}
KTILES = [c for c in ROPES if c[0][0] == "k"]
KT_AT = {c: i for i, c in enumerate(KTILES)}
N_KI = ROPE_AT[("qi", 3)] + 1


def ring(c):
    return RING_AT[c] if c < C_OUT else c - KC


def ring_before(c):
    r = ring(c) - RING
    return IN_RING[r] if r < len(IN_RING) else r + KC


def slot(c):
    return ring(c) % RING


def raw_slot(c):
    return (c - N_ADA0) % RAW


def split_after(c):
    r = ring(c)
    last = [IN_RING[i] if i < len(IN_RING) else i + KC for i in (r + RING - 1, r + RING)]
    return range(last[0] + 1, last[1] + 1)


def schedule():
    s = []
    for c in ROPES[:N_KI]:
        s += [("part", AT[c], 0, KC), ("end", AT[c]), ("split", AT[c])]
    s += [("vload",)]
    rounds = [(t, r) for t in (4, 3, 2, 0) for r in range(ROUNDS[t])]

    def topk(k):
        nonlocal s, rounds
        s += [("topk",) + r for r in rounds[:k]]
        rounds = rounds[k:]

    for t in (4, 3, 2, 0, 1):
        s += [("v", t)]
        if t != 1:
            s += [("idx", t, h) for h in range(IH)] + [("idxmask", t)]
        topk(5)
    for c in (("kb", 0), ("qb", 0)):
        s += [("part", AT[c], 0, KC), ("end", AT[c]), ("split", AT[c])]
        topk(5)
    fill = {u: [] for u in range(NU + 2)}

    def spread(c, periods):
        n = len(periods)
        for i, u in enumerate(periods):
            for k in range(KC * i // n, KC * (i + 1) // n):
                fill[u] += [("part", c, k, k + 1)] + ([("end", c)] if k == KC - 1 else [])

    for g in range(NG):
        u = 5 * g
        chunks = [AT[c] for c in group_chunks(g)]
        for i, c in enumerate(chunks):
            spread(c, (u, u + 1) if i == 0 else (u + 2, u + 3))
        if g == 4:
            fill[u + 2] += [("otr", h, 4 + h) for h in range(4)]
        if g > 4:
            fill[u + 2] += [("otr", g - 5, g - 5)]
        ada = [("ada", AT[("ada", 4 + g, q)]) for q in range(4)]
        if g < 4:
            fill[u + 4] += ada
        else:
            fill[u + 3] += ada[:2]
            fill[u + 4] += ada[2:]
    spread(AT[("gb", 0)], (NU, NU + 1))
    for g in range(NG):
        fill[5 * g + 5].insert(1, ("adarow", 4 + g))
    waiting = []
    for u in range(NU + 2):
        cut = (len(fill[u]) + 1) // 2
        if 0 < u <= NU:
            s += [("comb", u - 1)]
        if u < NU:
            s += [("qk", u)]
        if u == 22:
            s += [("bscale",)]
        for part, half in ((fill[u][:cut], 0), (fill[u][cut:], 1)):
            s += part
            waiting += [x[1] for x in part if x[0] == "end" and CH[x[1]] in ROPE_AT]
            if 0 < u <= NU and (half == 0 or u > 20):
                s += [("tr", u - 1, half)]
            if half == 0:
                if u < NU:
                    s += [("exp", u)]
                s += [("split", c) for c in waiting]
                waiting = []
                if u >= 2:
                    s += [("pv", u - 2)]
        if u == 21:
            s += [("bnorm",)]
        topk(-(-len(rounds) // (20 - u)) if u < 19 else len(rounds))
    s += [("otr", 3, 3)]
    assert not rounds and not waiting
    return s


def sets_before(u):
    return u if u <= 20 else 20 + 2 * (u - 20)


def build(nc, a, o):
    with ExitStack() as ctx:
        base = -(-nc.sbuf_base // 64) * 64
        at = {"x": base}

        def sb(name, shape, dt=F32, where=None):
            n = int(np.prod(shape[1:])) * 4
            off = where
            if where is None:
                off = at["x"]
                at["x"] += -(-n // 32) * 32
            assert off + n <= nc.sbuf_usable_end, name
            return nc.alloc_sbuf_tensor_at(name, shape, dt, offset=off), off + n

        cos, _ = sb("cos", [P, T])
        sin, _ = sb("sin", [P, T])
        off_cos, off_sin = base, base + T * 4
        off_cs = at["x"]
        cstat, _ = sb("cstat", [P, KC * 4 + P - 4], F32R)
        cs4 = cstat[:, 0:KC * 4].rearrange("p (k f) -> p k f", f=4)
        row, _ = sb("row", [P, 512])
        ident, _ = sb("ident", [P, P])
        ones, _ = sb("ones", [P, P])
        ada, _ = sb("ada", [P, 48, 2])
        bada, _ = sb("bada", [P, 48, 2])
        gains, _ = sb("gains", [P, 4, KC])
        gs, _ = sb("gs", [P, 2, KC, 2])
        gg, _ = sb("gg", [P, 2, KC, 2])
        ct, _ = sb("ct", [P, KC, 2])
        cf, _ = sb("cf", [P, KC, 2])
        hmask, _ = sb("hmask", [P, 2])
        wis, _ = sb("wis", [P, 5, IH])
        lam, _ = sb("lam", [P, 3])
        eps, _ = sb("eps", [P, 1])
        mx, _ = sb("mx", [P, NU, 2])
        nmx, _ = sb("nmx", [P, NU, 2])
        esum, _ = sb("esum", [P, NU, 2])
        rsum, _ = sb("rsum", [P, NU, 2])
        nlr, _ = sb("nlr", [P, 20])
        osq, _ = sb("osq", [P, 20])
        orms, _ = sb("orms", [P, 20])
        top8, _ = sb("top8", [P, 8])
        t4, _ = sb("t4", [P, 4, 4])
        raw_off = at["x"]
        raw, _ = sb("raw", [P, RAW, 1024])
        rawd, _ = sb("rawd", [P, 2, BLK_DOWN * P], where=raw_off)
        off_whi = at["x"]
        whi, _ = sb("whi", [P, RING, 1024], F32R)
        off_wlo = at["x"]
        wlo, _ = sb("wlo", [P, RING, 1024], F32R)
        off_d = ((RING * 1024 - BLK_DOWN * P) * 4, (RING * 1024 - 2 * BLK_DOWN * P) * 4)
        assert slot(C_DN - 1) == 0 and off_d[0] >= 4096 and off_d[1] >= 0
        dhi = [sb(f"dhi{k}", [P, BLK_DOWN * P], F32R, off_whi + off_d[k])[0] for k in range(2)]
        dlo = [sb(f"dlo{k}", [P, BLK_DOWN * P], F32R, off_wlo + off_d[k])[0] for k in range(2)]
        h_off = at["x"]
        hh, e1 = sb("hh", [P, KC, T], F32R)
        hl, _ = sb("hl", [P, KC, T], F32R)
        ymix, _ = sb("ymix", [P, KC, T], where=h_off)
        xres, _ = sb("xres", [P, KC, T], where=h_off + KC * T * 4)
        A0 = at["x"]
        A1 = A0 + KC * T * 4 * 1 + 2 * FC * T * 4
        assert A1 <= nc.sbuf_usable_end, (A1, nc.sbuf_usable_end)
        qi_h, n = sb("qi_h", [P, 4, T], F32R, A0)
        qi_l, n = sb("qi_l", [P, 4, T], F32R, n)
        oT, _ = sb("oT", [P, KC, T], F32, A0)
        ki, e = sb("ki", [P, 2, 2, KEYS], F32R, n)
        ob, _ = sb("ob", [P, 20, P], F32, n)
        kz0, n = sb("kz0", [P, 2, 2, KEYS], F32R, e)
        kz1, n = sb("kz1", [P, 2, 2, KEYS], F32R, n)
        off_q0 = n
        q0, n = sb("q0", [P, 2, T], F32R, n)
        q1, n = sb("q1", [P, 2, T], F32R, n)
        pt, pe_ = sb("pt", [P, 3, 512], F32, n)
        wv_h, n = sb("wv_h", [P, KC, VWI], F32R, e)
        wv_l, n = sb("wv_l", [P, KC, VWI], F32R, n)
        n = max(n, pe_)
        v_off = n
        vt, n = sb("vt", [P, 7, VWI], F32, n)
        mb, n = sb("mb", [P, MBOFF[4] + NKEY[4]], F32, n)
        e_off = n
        ee, n = sb("ee", [P, 2, 2, 512], F32, n)
        z, n = sb("z", [P, T], F32, n)
        zc, n = sb("zc", [P, T], F32, n)
        zs, n = sb("zs", [P, T], F32, n)
        ro, n = sb("ro", [P, 2, KEYS], F32, n)
        on, n = sb("on", [P, P], F32, n)
        assert n <= nc.sbuf_usable_end, n
        raw0, n = sb("raw0", [P, RAW0, 1024], F32, A0)
        assert n <= e
        xt, n = sb("xt", [P, KC, T], F32, v_off)
        lamv, n = sb("lamv", [P, 4, HD], F32, n)
        sq0, n = sb("sq0", [P, 2, T], F32, n)
        hf0, n = sb("hf0", [P, 2, T], F32, n)
        rstd0, n = sb("rstd0", [P, T], F32, n)
        rms0, n = sb("rms0", [P, T], F32, n)
        assert n <= nc.sbuf_usable_end
        mh, n = sb("mh", [P, KC, T], F32R, A0)
        ml, n = sb("ml", [P, KC, T], F32R, n)
        off_oth = n
        oth, n = sb("oth", [P, KC, T], F32R, n)
        assert n <= off_q0
        gate0, n = sb("gate0", [P, 2, T], F32, off_q0)
        otl, n = sb("otl", [P, KC, T], F32R, n)
        mt, n = sb("mt", [P, T], F32, n)
        gate1, n = sb("gate1", [P, 2, T], F32, n)
        gates = (gate0, gate1)
        x1, _ = sb("x1", [P, KC, T], F32, A0)
        sq1, n = sb("sq1", [P, 2, T], F32, off_oth)
        xr1, n = sb("xr1", [P, 2, T], F32, n)
        hf1, n = sb("hf1", [P, 2, T], F32, n)
        rstd1, n = sb("rstd1", [P, T], F32, n)
        rms1, n = sb("rms1", [P, T], F32, n)
        rstd2, n = sb("rstd2", [P, T], F32, n)
        acc1, _ = sb("acc1", [P, T], F32, off_cs)
        acc2, _ = sb("acc2", [P, T], F32, off_cs)
        fh, n = sb("fh", [P, FC, T], F32R, A0 + KC * T * 4)
        fl, n = sb("fl", [P, FC, T], F32R, n)
        assert n <= A1
        ft, _ = sb("ft", [P, T], F32, off_cos)
        sg, _ = sb("sg", [P, T], F32, off_sin)
        sq2, _ = sb("sq2", [P, T], F32, off_cos)
        rstd3, _ = sb("rstd3", [P, T], F32, off_sin)
        hh2 = nc.alloc_sbuf_tensor_at("hh2", [P, KC, T], F32R, offset=h_off)
        hl2 = nc.alloc_sbuf_tensor_at("hl2", [P, KC, T], F32R, offset=h_off + KC * T * 4)

        def pb(name, shape):
            return ctx.enter_context(nc.psum_tensor(name, shape, F32))

        pj = [pb("pj0", [P, 2, 512]), pb("pj1", [P, 2, 512])]
        lg = pb("lg", [P, 2, 512])
        tb = pb("tb", [P, 512])
        pvb = pb("pvb", [P, 512])

        def sem(name):
            return ctx.enter_context(nc.semaphore(name))

        c_in, misc_in, trig_in, vcache_in = sem("c_in"), sem("misc_in"), sem("trig_in"), sem("vcache_in")
        xres_in = sem("xres_in")
        raw0_in = [sem(f"raw0_in{i}") for i in range(RAW0)]
        raw_in = [sem(f"raw_in{i}") for i in range(RAW)]
        x_in = sem("x_in")
        down_in = [sem(f"down_in{i}") for i in range(2)]
        cache_in = [sem(f"cache_in{i}") for i in range(len(KTILES))]
        k_out = [sem(f"k_out{i}") for i in range(len(KTILES))]
        vp_out, vs_out = sem("vp_out"), sem("vs_out")
        y_out = sem("y_out")
        w_hi = sem("w_hi")
        w_lo = sem("w_lo")
        w_lo_dve = sem("w_lo_dve")
        ada_used = sem("ada_used")
        down_used = sem("down_used")
        pj_full = sem("pj_full")
        pj_act = sem("pj_act")
        pj_dve = sem("pj_dve")
        consts = sem("consts")
        c_silu, c_hi, c_lo = sem("c_silu"), sem("c_hi"), sem("c_lo")
        ada_sb, ada_done = sem("ada_sb"), sem("ada_done")
        sq_ready, sq_used, rstd_ready = sem("sq_ready"), sem("sq_used"), sem("rstd_ready")
        xr_ready, hf_ready, h_hi, h_lo = sem("xr_ready"), sem("hf_ready"), sem("h_hi"), sem("h_lo")
        zc_ready, rope_o, rope_hi, rope_lo = sem("zc_ready"), sem("rope_o"), sem("rope_hi"), sem("rope_lo")
        dve = sem("dve")
        ix_full, ix_relu, ix_acc = sem("ix_full"), sem("ix_relu"), sem("ix_acc")
        lam_dots, lam_exp = sem("lam_dots"), sem("lam_exp")
        qk_ready, mx_ready, e_ready, p_ready = sem("qk_ready"), sem("mx_ready"), sem("e_ready"), sem("p_ready")
        tr_ready, pt_ready, pt_used, o_ready = (sem("tr_ready"), sem("pt_ready"), sem("pt_used"),
                                                sem("o_ready"))
        on_rms, on_ready = sem("on_rms"), sem("on_ready")
        ot_hi, ot_lo = sem("ot_hi"), sem("ot_lo")
        m_ready, m_hi, m_lo = sem("m_ready"), sem("m_hi"), sem("m_lo")
        ysq_ready, acc_ready, acc_zero = sem("ysq_ready"), sem("acc_ready"), sem("acc_zero")
        yg_ready, x1_dve, x1_pool = sem("yg_ready"), sem("x1_dve"), sem("x1_pool")
        f_hi, f_lo = sem("f_hi"), sem("f_lo")
        y_fin = sem("y_fin")

        SCHED = schedule()

        takers = []
        tile_of = {}

        def tile(who, *names):
            for name in names:
                tile_of[name] = len(takers)
            takers.append(who)

        for n in range(N_ADA0 // 4):
            if n == 1:
                tile("A", "stat0")
            tile("D", ("ada", n))
        for s in SCHED:
            if s[0] == "end":
                tile("A", s[1])
            elif s[0] == "v":
                tile("A", ("v", s[1]))
            elif s[0] == "adarow":
                tile("D", ("ada", s[1]))
            elif s[0] == "otr":
                tile("D", ("otr", s[2]))
        for d in range(KC):
            if d + 1 < KC:
                tile("A", AT[("ga", d + 1)])
                tile("A", AT[("gb", d + 1)])
            tile("D", ("oa", d))
            tile("D", ("ob", d))
        T_OUT = len(takers)
        takers += ["A"] * KC
        tile_of["stat1"] = len(takers); takers.append("A")
        tile_of["stat2"] = len(takers); takers.append("A")
        T_GU = len(takers)
        takers += ["A", "D"] * FC
        T_DN = len(takers)
        takers += ["A"] * KC
        tile_of["stat3"] = len(takers); takers.append("A")

        def taken(n, who):
            return takers[:n + 1].count(who)

        def pj_free(pe, n):
            if n >= 2:
                who = takers[n - 2]
                pe.wait_ge(pj_act if who == "A" else pj_dve, taken(n - 2, who))

        def two(ap):
            return ap.rearrange("p (a b) -> p a b", a=2)

        def pj_view(n):
            return pj[n % 2][:, :, 0:HALF]

        def in_dve(c):
            return c < N_ADA0

        def lo_count(c):
            return c + 1 - N_ADA0

        def wait_lo(eng, c):
            if in_dve(c):
                eng.wait_ge(w_lo_dve, c + 1)
            else:
                eng.wait_ge(w_lo, lo_count(c))

        def wait_raw(eng, c):
            if c < N_ADA0:
                eng.wait_ge(raw0_in[c % RAW0], 16 * (c // RAW0 + 1))
            else:
                eng.wait_ge(raw_in[raw_slot(c)], 16 * ((c - N_ADA0) // RAW + 1))

        def raw_of(c):
            return raw0[:, c % RAW0, :] if c < N_ADA0 else raw[:, raw_slot(c), :]

        def wait_used(eng, c, turns=None, chunks=0):
            if c >= C_DN:
                d, k = divmod(c - C_DN, 2)
                if k == 0:
                    eng.wait_ge(down_used, d + 1)
                    return
                tile = T_DN + d
            elif c >= C_GU:
                tile = T_GU + c - C_GU
            elif c >= C_OUT:
                tile = T_OUT + c - C_OUT
            elif CH[c][0] == "ada":
                eng.wait_ge(ada_used, sum(x[0] == "ada" for x in CH[:c + 1]))
                return
            elif CH[c][0] == "wo":
                tile = tile_of[("ob", CH[c][1])]
            else:
                tile = tile_of[c]
            eng.wait_ge(pj_full, tile + 1 if turns is None else turns * chunks + (tile + 1))

        def slot_free(eng, c):
            if ring(c) >= RING:
                wait_used(eng, ring_before(c))

        def kz_of(c):
            name, j = c
            return ki if name == "ki" else (kz1 if name == "kb" and j % 2 else kz0)

        def q_of(c):
            name, j = c
            if name == "qi":
                return qi_h[:, j, :], qi_l[:, j, :]
            t = q1 if j % 2 else q0
            return t[:, 0, :], t[:, 1, :]

        def rope_dst_free(eng, c):
            name, j = c
            if name == "kb":
                if j < 2:
                    eng.wait_ge(pj_full, tile_of[("v", 1)] + 1)
                else:
                    eng.wait_ge(qk_ready, 5 * (j - 1))
            elif name == "qb":
                if j >= 2:
                    eng.wait_ge(qk_ready, 5 * (j - 1))
            elif name == "ka":
                eng.wait_ge(qk_ready, 15)
            elif name == "qa":
                eng.wait_ge(qk_ready, 5 * (3 + j))

        def unit(u):
            g, t = divmod(u, 5)
            return g, t, g < 4

        def last_rope(g):
            return ROPE_AT[("qb", g)] if g < 4 else ROPE_AT[("qa", g - 4)]

        block = ctx.enter_context(nc.Block())

        @block.sync
        def _(sp):
            def load(c):
                if c < N_ADA0:
                    if c >= RAW0:
                        sp.wait_ge(w_lo_dve, c - RAW0 + 1)
                    sp.dma_start(raw_of(c), a["w_ada"][c]).then_inc(raw0_in[c % RAW0], 16)
                    return
                if c >= N_ADA0 + RAW:
                    sp.wait_ge(w_lo, lo_count(c - RAW))
                name = CH[c] if c < C_OUT else None
                if name is None:
                    src = a["w_s"][S_OUT + c - C_OUT]
                elif name[0] == "v":
                    src = a["w_v"][name[1]]
                elif name[0] == "ada":
                    src = a["w_ada"][name[1] * 4 + name[2]]
                else:
                    src = a["w_s"][W_ROW[name]]
                dst = raw[:, raw_slot(c), 0:VWI if name and name[0] == "v" else 1024]
                sp.dma_start(dst, src).then_inc(raw_in[raw_slot(c)], 16)

            def load_keys(k):
                r = ROPE_AT[k]
                if r >= 2:
                    sp.wait_ge(rope_hi, r - 1)
                    sp.wait_ge(rope_lo, r - 1)
                    if ROPES[r - 2] in KT_AT:
                        sp.wait_ge(k_out[KT_AT[ROPES[r - 2]]], 16)
                sp.dma_start(ro[:, r % 2, 0:PAST], a["cache_k"][KT_AT[k]]).then_inc(cache_in[KT_AT[k]], 16)

            sp.dma_start(ct[:, :, :], a["cT"]).then_inc(c_in, 16)
            load(0)
            for dst, src in ((ident, "ident"), (bada, "bada"), (gains, "gains"), (lamv, "lamv"), (hmask, "hmask")):
                sp.dma_start(dst[...], a[src]).then_inc(misc_in, 16)
            for c in range(1, RAW0):
                load(c)
            sp.dma_start(xt[:, :, :], a["xT"]).then_inc(x_in, 16)
            for c in range(RAW0, N_ADA0 + 3):
                load(c)
            sp.dma_start(cos[:, :], a["cos"]).then_inc(trig_in, 16)
            sp.dma_start(sin[:, :], a["sin"]).then_inc(trig_in, 16)
            for c in range(N_ADA0 + 3, C_OUT + 4):
                load(c)
                if c == AT[("v", 3)]:
                    sp.wait_ge(h_lo, KC)
                    load_keys(KTILES[0])
                    sp.dma_start(vt[:, 0:2, 0:VW], a["cache_v"]).then_inc(vcache_in, 16)
                if c - 2 > AT[KTILES[0]] and c - 2 < C_OUT and CH[c - 2] in KT_AT:
                    load_keys(CH[c - 2])
            wait_used(sp, AT[("gb", KC - 1)])
            sp.dma_start(xres[:, :, :], a["xT"]).then_inc(xres_in, 16)
            with sp.Fori(0, (C_DN - C_OUT - 4) // (2 * RAW)) as i:
                for k in range(2 * RAW):
                    c = C_OUT + 4 + k
                    sp.wait_ge(w_lo, i * (2 * RAW) + lo_count(c - RAW))
                    sp.dma_start(raw[:, raw_slot(c), :], a["w_s"][bass.ds(i * (2 * RAW) + (S_OUT + 4 + k), 1)]
                                 .rearrange("a p n -> p (a n)")).then_inc(raw_in[raw_slot(c)], 16)
            sp.wait_ge(w_lo, lo_count(C_DN - 1))
            for k in range(2):
                sp.dma_start(rawd[:, k, :], a["w_d"][k]).then_inc(down_in[k], 16)
            with sp.Fori(0, KC - 1) as i:
                for k in range(2):
                    sp.wait_ge(w_lo, i * 2 + (lo_count(C_DN + k)))
                    sp.dma_start(rawd[:, k, :], a["w_d"][bass.ds(i * 2 + (2 + k), 1)]
                                 .rearrange("a p n -> p (a n)")).then_inc(down_in[k], 16)
            for kc in range(KC):
                sp.wait_ge(y_fin, kc + 1)
                sp.dma_start(o["yT"][kc], x1[:, kc, :]).then_inc(y_out, 16)
            sp.wait_ge(y_out, 16 * KC)
            sp.wait_ge(vp_out, 16)
            sp.wait_ge(vs_out, 16)
            for s in k_out:
                sp.wait_ge(s, 16)

        @block.scalar
        def _(act):
            def hi(c):
                wait_raw(act, c)
                if c < C_OUT and CH[c][0] == "v":
                    dst, src = wv_h[:, CH[c][1], :], raw[:, raw_slot(c), 0:VWI]
                else:
                    slot_free(act, c)
                    dst, src = whi[:, slot(c), :], raw_of(c)
                act.activation(dst, src, ACT.Copy).then_inc(w_hi, 1)

            def hi_after(c):
                for x in split_after(c):
                    hi(x)

            act.wait_ge(c_in, 16)
            act.activation(cf[:, :, :], ct[:, :, :], ACT.Silu).then_inc(c_silu, 1)
            act.wait_ge(consts, 3)
            act.wait_ge(c_silu, 1)
            act.activation(cs4[:, :, 0:2], cf[:, :, :], ACT.Copy).then_inc(c_hi, 1)
            for c in range(RING):
                hi(c)

            def rows(n):
                act.wait_ge(ada_used, 4 * (n + 1))
                tile = tile_of[("ada", n)]
                if n:
                    act.wait_ge(pj_full, tile_of[("ada", n - 1)] + 1)
                act.activation(row[0:4, :], pj[tile % 2][0:4, 0, :], ACT.Copy).then_inc(ada_sb, 1)

            def squares(src, sq, first):
                for kc in range(KC):
                    if first + kc >= 2:
                        act.wait_ge(sq_used, first + kc - 1)
                    act.activation(sq[:, kc % 2, :], src[:, kc, :], ACT.Square).then_inc(sq_ready, 1)

            def rms(tile, dst, n):
                act.wait_ge(pj_full, tile + 1)
                act.wait_ge(consts, 3)
                act.activation(two(dst[:, :]), pj_view(tile), ACT.Sqrt, bias=eps[:, 0:1], scale=1.0 / D)\
                   .then_inc(pj_act, 1)

            for c in range(N_ADA0 - 2):
                if c == RAW0 - RING:
                    act.wait_ge(x_in, 16)
                    squares(xt, sq0, 0)
                    rms(tile_of["stat0"], rms0, 0)
                hi_after(c)
                if c % 4 == 3:
                    rows(c // 4)
            rows(N_ADA0 // 4 - 1)
            ahead = [*split_after(N_ADA0 - 2), *split_after(N_ADA0 - 1)]
            for kc in range(KC):
                act.wait_ge(hf_ready, kc + 1)
                act.activation(hh[:, kc, :], hf0[:, kc % 2, :], ACT.Copy).then_inc(h_hi, 1)
                if kc in (2, 4):
                    hi(ahead.pop(0))
            for c in ahead:
                hi(c)
            act.wait_ge(lam_dots, 1)
            act.activation(lam[:, 0:2], lam[:, 0:2], ACT.Exp).then_inc(lam_exp, 1)

            def rope_evac(c):
                n, r = tile_of[c], ROPE_AT[CH[c]]
                act.wait_ge(pj_full, n + 1)
                if r == 0:
                    act.wait_ge(h_lo, KC)
                if r >= 1:
                    act.wait_ge(rope_o, r)
                act.activation(two(z[:, :]), pj_view(n), ACT.Copy).then_inc(pj_act, 1)

            def rope_split(c):
                name = CH[c]
                r = ROPE_AT[name]
                act.wait_ge(rope_o, r + 1)
                rope_dst_free(act, name)
                if name in KT_AT:
                    k = KT_AT[name]
                    act.dma_start(o["kT"][k], ro[:, r % 2, PAST:KEYS]).then_inc(k_out[k], 16)
                    act.wait_ge(cache_in[k], 16)
                    dst = kz_of(name)
                    for m in range(2):
                        ins = act.activation(dst[:, 0, m, :], ro[:, r % 2, :], ACT.Copy, scale=hmask[:, m:m + 1])
                    ins.then_inc(rope_hi, 1)
                else:
                    act.activation(q_of(name)[0], ro[:, r % 2, PAST:KEYS], ACT.Copy).then_inc(rope_hi, 1)

            def gate(name, d):
                n = tile_of[AT[(name, d)]]
                act.wait_ge(pj_full, n + 1)
                if d >= 2:
                    act.wait_ge(m_ready, d - 1)
                act.activation(two(gates[d % 2][:, 0 if name == "ga" else 1, :]), pj_view(n), ACT.Sigmoid)\
                   .then_inc(pj_act, 1)

            ix = 0
            sets = 0
            for s in SCHED:
                if s[0] == "end":
                    c = s[1]
                    if CH[c] in ROPE_AT:
                        rope_evac(c)
                    else:
                        gate(*CH[c])
                    hi_after(c)
                elif s[0] == "split":
                    rope_split(s[1])
                elif s[0] == "ada":
                    hi_after(s[1])
                elif s[0] == "adarow":
                    rows(s[1])
                elif s[0] == "v":
                    t = s[1]
                    act.wait_ge(pj_full, tile_of[("v", t)] + 1)
                    blk = 2 if t == 0 else 2 + t
                    act.activation(two(vt[:, blk, :]), pj[tile_of[("v", t)] % 2][:, :, 0:VH], ACT.Copy)\
                       .then_inc(pj_act, 1)
                    act.wait_ge(pj_act, taken(tile_of[("v", t)], "A"))
                    if t == 0:
                        act.dma_start(o["v_s"], vt[0:NS, 2, 0:VW]).then_inc(vs_out, 16)
                elif s[0] == "idx":
                    t = s[1]
                    act.wait_ge(ix_full, ix + 1)
                    if ix >= 2:
                        act.wait_ge(ix_acc, ix - 1)
                    act.activation(ee[:, 0, ix % 2, 0:NKEY[t]], lg[:, ix % 2, 0:NKEY[t]], ACT.Relu)\
                       .then_inc(ix_relu, 1)
                    ix += 1
                elif s[0] == "exp":
                    u = s[1]
                    g, t, diff = unit(u)
                    if u == 0:
                        act.wait_ge(ix_acc, 32)
                    act.wait_ge(mx_ready, u + 1)
                    for m in range(2):
                        src = lg[:, m, 0:NKEY[t]] if diff else ee[:, u % 2, m, 0:NKEY[t]]
                        ins = act.activation(ee[:, u % 2, m, 0:NKEY[t]], src, ACT.Exp, bias=nmx[:, u, m:m + 1],
                                             scale=SCALE, accum_out=esum[:, u, m:m + 1])
                    ins.then_inc(e_ready, 1)
                elif s[0] == "tr" and not (s[2] and s[1] < 20):
                    g, t, diff = unit(s[1])
                    act.wait_ge(tr_ready, sets + 1)
                    if sets >= 3:
                        act.wait_ge(pt_used, sets - 2)
                    act.activation(pt[:, sets % 3, 0:NBLK[t] * P], tb[:, 0:NBLK[t] * P], ACT.Copy)\
                       .then_inc(pt_ready, 1)
                    sets += 1
                elif s[0] == "bnorm":
                    act.wait_ge(o_ready, 20)
                    act.activation(orms[:, :], osq[:, :], ACT.Sqrt, bias=eps[:, 0:1], scale=1.0 / P)\
                       .then_inc(on_rms, 1)
            act.wait_ge(pj_dve, taken(tile_of[("otr", 3)], "D"))
            for out_sem in (vp_out, vs_out, *k_out):
                act.wait_ge(out_sem, 16)
            for kc in range(KC):
                act.activation(oth[:, kc, :], oT[:, kc, :], ACT.Copy).then_inc(ot_hi, 1)
            for d in range(KC):
                if d + 1 < KC:
                    for name in ("ga", "gb"):
                        gate(name, d + 1)
                        hi_after(AT[(name, d + 1)])
                act.wait_ge(m_ready, d + 1)
                act.activation(mh[:, d, :], mt[:, :], ACT.Copy).then_inc(m_hi, 1)
                hi_after(AT[("wo", d)])
            for d in range(KC):
                n = T_OUT + d
                act.wait_ge(pj_full, n + 1)
                if d == 0:
                    wait_used(act, AT[("gb", KC - 1)])
                act.activation(two(ymix[:, d, :]), pj_view(n), ACT.Copy).then_inc(pj_act, 1)
                hi_after(C_OUT + d)
                if d >= 2:
                    act.wait_ge(acc_ready, d - 1)
                act.wait_ge(pj_act, taken(n, "A"))
                if d == 0:
                    wait_used(act, C_OUT - 1)
                act.activation(sq1[:, d % 2, :], ymix[:, d, :], ACT.Square).then_inc(ysq_ready, 1)
            act.wait_ge(consts, 3)
            rms(tile_of["stat1"], rms1, 1)
            for kc in range(KC):
                if kc % 2:
                    act.wait_ge(x1_dve, kc // 2 + 1)
                else:
                    act.wait_ge(x1_pool, kc // 2 + 1)
                if kc < 2:
                    act.wait_ge(acc_ready, KC)
                else:
                    act.wait_ge(sq_used, KC - 1 + kc - 1)
                act.activation(sq1[:, kc % 2, :], x1[:, kc, :], ACT.Square).then_inc(sq_ready, 1)
            act.wait_ge(rstd_ready, 2)
            rms(tile_of["stat2"], rms1, 2)
            for kc in range(KC):
                act.wait_ge(hf_ready, KC + kc + 1)
                act.activation(hh2[:, kc, :], hf1[:, kc % 2, :], ACT.Copy).then_inc(h_hi, 1)
            def gu(i, t0, n_tiles):
                for t in range(t0, t0 + n_tiles):
                    n = T_GU + 2 * t
                    act.wait_ge(pj_full, i * 6 + (n + 1))
                    if t:
                        act.wait_ge(pj_dve, i * 3 + taken(n - 1, "D"))
                    act.activation(two(sg[:, :]), pj_view(n), ACT.Silu).then_inc(pj_act, 1)
                    for k in range(2):
                        c = C_GU + 2 * t + k + RING
                        if c < C_DN:
                            act.wait_ge(raw_in[raw_slot(c)], i * 32 + 16 * ((c - N_ADA0) // RAW + 1))
                            wait_used(act, c - RING, i, 6)
                            act.activation(whi[:, slot(c), :], raw[:, raw_slot(c), :], ACT.Copy).then_inc(w_hi, 1)
                    act.wait_ge(pj_dve, i * 3 + taken(n + 1, "D"))
                    act.activation(fh[:, bass.ds(i * 3 + t, 1), :].rearrange("p a n -> p (a n)"),
                                   ft[:, :], ACT.Copy).then_inc(f_hi, 1)

            gu(0, 0, 1)
            with act.Fori(0, FC // 3 - 1) as i:
                gu(i, 1, 3)
            gu(0, FC - 3, 3)

            def hi_down(d, k):
                act.wait_ge(down_in[k], 16 * (d + 1))
                wait_used(act, C_DN + 2 * d + k - 2)
                act.activation(dhi[k][:, :], rawd[:, k, :], ACT.Copy).then_inc(w_hi, 1)

            hi_down(0, 0)
            hi_down(0, 1)
            for d in range(KC):
                n = T_DN + d
                if d < KC - 1:
                    hi_down(d + 1, 0)
                    hi_down(d + 1, 1)
                act.wait_ge(pj_full, n + 1)
                act.activation(two(ymix[:, d, :]), pj_view(n), ACT.Copy).then_inc(pj_act, 1)
                act.wait_ge(acc_ready, KC + d)
                act.wait_ge(pj_act, taken(n, "A"))
                if d == 0:
                    act.wait_ge(f_lo, FC)
                act.activation(sq2[:, :], ymix[:, d, :], ACT.Square).then_inc(ysq_ready, 1)
            act.wait_ge(acc_ready, 2 * KC)
            n = tile_of["stat3"]
            act.wait_ge(pj_full, n + 1)
            act.activation(two(sq2[:, :]), pj_view(n), ACT.Sqrt, bias=eps[:, 0:1], scale=1.0 / D).then_inc(pj_act, 1)

        @block.gpsimd
        def _(pool):
            pool.memset(cstat[:, :].bitcast(F32), 0.0).then_inc(consts, 1)
            pool.memset(ones[:, :], 1.0).then_inc(consts, 1)
            pool.memset(eps[:, :], EPS).then_inc(consts, 1)

            def lo(c):
                wait_raw(pool, c)
                pool.wait_ge(w_hi, c + 1)
                if c < C_OUT and CH[c][0] == "v":
                    dst, h, src = wv_l[:, CH[c][1], :], wv_h[:, CH[c][1], :], raw[:, raw_slot(c), 0:VWI]
                else:
                    slot_free(pool, c)
                    dst, h, src = wlo[:, slot(c), :], whi[:, slot(c), :], raw_of(c)
                pool.tensor_tensor(dst, src, h.bitcast(F32), ALU.subtract).then_inc(w_lo, 1)

            def lo_after(c):
                for x in split_after(c):
                    lo(x)

            pool.wait_ge(rstd_ready, 1)
            for kc in range(KC):
                pool.tensor_tensor(xt[:, kc, :], xt[:, kc, :], rstd0[:, :], ALU.mult).then_inc(xr_ready, 1)
            for c in (N_ADA0 - 3, N_ADA0 - 2, N_ADA0 - 1):
                lo_after(c)
            pool.wait_ge(trig_in, 32)
            for s in SCHED:
                if s[0] == "end":
                    c = s[1]
                    if CH[c] in ROPE_AT:
                        r = ROPE_AT[CH[c]]
                        pool.wait_ge(pj_act, taken(tile_of[c], "A"))
                        if r >= 1:
                            pool.wait_ge(rope_o, r)
                        pool.tensor_tensor(zc[:, :], z[:, :], cos[:, :], ALU.mult).then_inc(zc_ready, 1)
                    lo_after(c)
                elif s[0] == "ada":
                    lo_after(s[1])
                elif s[0] == "v" and s[1] == 1:
                    pool.wait_ge(pj_act, taken(tile_of[("v", 1)], "A"))
                    pool.dma_start(o["v_p"], vt[:, 3:7, 0:VW]).then_inc(vp_out, 16)
            for d in range(KC):
                if d + 1 < KC:
                    lo_after(AT[("ga", d + 1)])
                    lo_after(AT[("gb", d + 1)])
                pool.wait_ge(m_hi, d + 1)
                pool.tensor_tensor(ml[:, d, :], mt[:, :], mh[:, d, :].bitcast(F32), ALU.subtract).then_inc(m_lo, 1)
                lo_after(AT[("wo", d)])
            pool.wait_ge(ada_done, 12)
            pool.memset(acc1[:, :], 0.0).then_inc(acc_zero, 1)
            pool.wait_ge(acc_zero, 1)
            for d in range(KC):
                lo_after(C_OUT + d)
                pool.wait_ge(ysq_ready, d + 1)
                if d:
                    pool.wait_ge(acc_ready, d)
                pool.tensor_tensor(acc1[:, :], acc1[:, :], sq1[:, d % 2, :], ALU.add).then_inc(acc_ready, 1)
            pool.wait_ge(xres_in, 16)
            for kc in range(0, KC, 2):
                pool.wait_ge(yg_ready, kc + 1)
                pool.tensor_tensor(x1[:, kc, :], ymix[:, kc, :], xres[:, kc, :], ALU.add).then_inc(x1_pool, 1)
            pool.wait_ge(x1_dve, KC // 2)
            pool.wait_ge(x1_pool, KC // 2)
            pool.wait_ge(rstd_ready, 3)
            for kc in range(KC):
                if kc >= 2:
                    pool.wait_ge(hf_ready, KC + kc - 1)
                pool.tensor_tensor(xr1[:, kc % 2, :], x1[:, kc, :], rstd2[:, :], ALU.mult).then_inc(xr_ready, 1)

            def gu_lo(i, t0, n_tiles):
                for t in range(t0, t0 + n_tiles):
                    for k in range(2):
                        c = C_GU + 2 * t + k + RING
                        if c < C_DN:
                            pool.wait_ge(raw_in[raw_slot(c)], i * 32 + 16 * ((c - N_ADA0) // RAW + 1))
                            pool.wait_ge(w_hi, i * 6 + (c + 1))
                            wait_used(pool, c - RING, i, 6)
                            pool.tensor_tensor(wlo[:, slot(c), :], raw[:, raw_slot(c), :],
                                               whi[:, slot(c), :].bitcast(F32), ALU.subtract).then_inc(w_lo, 1)

            gu_lo(0, 0, 1)
            with pool.Fori(0, FC // 3 - 1) as i:
                gu_lo(i, 1, 3)
            gu_lo(0, FC - 3, 3)
            pool.wait_ge(pj_full, tile_of["stat1"] + 1)
            pool.memset(acc2[:, :], 0.0).then_inc(acc_zero, 1)
            pool.wait_ge(acc_zero, 2)

            def lo_down(d, k):
                pool.wait_ge(down_in[k], 16 * (d + 1))
                pool.wait_ge(w_hi, C_DN + 2 * d + k + 1)
                wait_used(pool, C_DN + 2 * d + k - 2)
                pool.tensor_tensor(dlo[k][:, :], rawd[:, k, :], dhi[k][:, :].bitcast(F32), ALU.subtract)\
                    .then_inc(w_lo, 1)

            lo_down(0, 0)
            lo_down(0, 1)
            for d in range(KC):
                if d < KC - 1:
                    lo_down(d + 1, 0)
                    lo_down(d + 1, 1)
                pool.wait_ge(ysq_ready, KC + d + 1)
                pool.wait_ge(acc_ready, KC + d)
                pool.tensor_tensor(acc2[:, :], acc2[:, :], sq2[:, :], ALU.add).then_inc(acc_ready, 1)

        @block.vector
        def _(v):
            chain = [0]

            def link(ins):
                chain[0] += 1
                ins.then_inc(dve, 1)
                v.wait_ge(dve, chain[0])

            v.wait_ge(consts, 3)
            v.wait_ge(c_hi, 1)
            v.tensor_tensor(cs4[:, :, 2:4], cf[:, :, :], cs4[:, :, 0:2].bitcast(F32), ALU.subtract).then_inc(c_lo, 1)

            def ada_columns(n):
                tile = tile_of[("ada", n)]
                v.wait_ge(pj_full, tile + 1)
                v.tensor_copy(t4[:, :, :], pj[tile % 2][:, 1, 0:16].rearrange("p (a b) -> p a b", a=4)).then_inc(pj_dve, 1)
                v.wait_ge(pj_dve, taken(tile, "D"))
                dst = ada[:, 4 * n:4 * n + 4, :]
                link(v.tensor_tensor(dst, t4[:, :, 0:2], t4[:, :, 2:4], ALU.add))
                v.tensor_tensor(dst, dst, bada[:, 4 * n:4 * n + 4, :], ALU.add).then_inc(ada_done, 1)

            def lo(c):
                wait_raw(v, c)
                v.wait_ge(w_hi, c + 1)
                v.tensor_tensor(wlo[:, slot(c), :], raw_of(c), whi[:, slot(c), :].bitcast(F32), ALU.subtract)\
                 .then_inc(w_lo_dve, 1)

            for c in range(RING):
                lo(c)
            v.wait_ge(misc_in, 16 * 5)
            link(v.tensor_tensor(lamv[:, 0:2, :], lamv[:, 0:2, :], lamv[:, 2:4, :], ALU.mult))
            v.tensor_reduce(lam[:, 0:2], lamv[:, 0:2, :], AX.X, ALU.add).then_inc(lam_dots, 1)
            for c in range(N_ADA0 - 1):
                if c + RING < N_ADA0:
                    lo(c + RING)
                if c % 4 == 3:
                    ada_columns(c // 4)
                if c == RAW0 - RING:
                    v.wait_ge(pj_act, taken(tile_of["stat0"], "A"))
                    v.reciprocal(rstd0[:, :], rms0[:, :]).then_inc(rstd_ready, 1)
            ada_columns(3)
            v.wait_ge(ada_done, 4)

            def gain_scale(n, sc):
                for w in range(2):
                    v.scalar_tensor_tensor(out=gs[:, n, :, w], in0=ada[:, sc:sc + KC, w], scalar=1.0,
                                           in1=gains[:, 2 * n, :], op0=ALU.add, op1=ALU.mult).then_inc(dve, 1)
                    chain[0] += 1
                v.wait_ge(dve, chain[0])

            gain_scale(0, KC)
            SPANS = ((1, 0, NS), (0, NS, T))

            def modulate(n, sh, xr, hf, hi_, lo_):
                for kc in range(KC + 1):
                    if kc < KC:
                        v.wait_ge(xr_ready, n * KC + kc + 1)
                        if kc >= 2:
                            v.wait_ge(h_lo, n * KC + kc - 1)
                        for w, c0, c1 in SPANS:
                            ins = v.tensor_scalar(hf[:, kc % 2, c0:c1], xr(kc)[:, c0:c1], gs[:, n, kc, w:w + 1],
                                                  ada[:, sh + kc, w:w + 1], ALU.mult, ALU.add)
                        ins.then_inc(hf_ready, 1)
                    if kc:
                        v.wait_ge(h_hi, n * KC + kc)
                        v.tensor_tensor(lo_[:, kc - 1, :], hf[:, (kc - 1) % 2, :], hi_[:, kc - 1, :].bitcast(F32),
                                        ALU.subtract).then_inc(h_lo, 1)

            modulate(0, 0, lambda kc: xt[:, kc, :], hf0, hh, hl)
            v.wait_ge(lam_exp, 1)
            link(v.tensor_tensor(lam[:, 2:3], lam[:, 0:1], lam[:, 1:2], ALU.subtract))
            link(v.tensor_scalar(lam[:, 2:3], lam[:, 2:3], -1.0, -LAM_INIT, ALU.mult, ALU.add))
            t1 = mb[:, MBOFF[1]:MBOFF[1] + NKEY[1]]
            link(v.memset(t1, 0.0))
            link(v.memset(mb[0:64, MBOFF[1] + 64:MBOFF[1] + P], NEG))

            v.wait_ge(trig_in, 32)

            def rope(c):
                r = ROPE_AT[CH[c]]
                v.wait_ge(pj_act, taken(tile_of[c], "A"))
                v.tensor_tensor(zs[64:128, :], z[0:64, :], sin[0:64, :], ALU.mult).then_inc(dve, 1)
                v.tensor_tensor(zs[0:64, :], z[64:128, :], sin[64:128, :], ALU.mult).then_inc(dve, 1)
                chain[0] += 2
                v.wait_ge(dve, chain[0])
                v.wait_ge(zc_ready, r + 1)
                if r >= 2:
                    v.wait_ge(rope_hi, r - 1)
                    v.wait_ge(rope_lo, r - 1)
                    if ROPES[r - 2] in KT_AT:
                        v.wait_ge(k_out[KT_AT[ROPES[r - 2]]], 16)
                v.tensor_tensor(ro[:, r % 2, PAST:KEYS], zc[:, :], zs[:, :], ALU.add).then_inc(rope_o, 1)

            def rope_lo_part(c):
                name = CH[c]
                r = ROPE_AT[name]
                v.wait_ge(rope_hi, r + 1)
                if name in KT_AT:
                    dst = kz_of(name)
                    for m in range(2):
                        ins = v.scalar_tensor_tensor(out=dst[:, 1, m, :], in0=ro[:, r % 2, :], scalar=hmask[:, m:m + 1],
                                                     in1=dst[:, 0, m, :].bitcast(F32), op0=ALU.mult, op1=ALU.subtract)
                    ins.then_inc(rope_lo, 1)
                else:
                    qh, ql = q_of(name)
                    v.tensor_tensor(ql, ro[:, r % 2, PAST:KEYS], qh.bitcast(F32), ALU.subtract).then_inc(rope_lo, 1)

            ix = 0
            for s in SCHED:
                if s[0] == "end" and CH[s[1]] in ROPE_AT:
                    rope(s[1])
                elif s[0] == "split":
                    rope_lo_part(s[1])
                elif s[0] == "adarow":
                    ada_columns(s[1])
                elif s[0] == "otr":
                    tile = tile_of[("otr", s[2])]
                    v.wait_ge(pj_full, tile + 1)
                    v.tensor_copy(oT[:, s[2], NS:T], pj[tile % 2][:, 0, :])
                    v.tensor_copy(oT[:, s[2], 0:NS], pj[tile % 2][:, 1, 0:NS]).then_inc(pj_dve, 1)
                elif s[0] == "v":
                    t = s[1]
                    v.wait_ge(pj_act, taken(tile_of[("v", t)], "A"))
                    link(v.tensor_scalar(wis[:, t, :], vt[:, 2 if t == 0 else 2 + t, VW:VWI], IDX_SCALE, None, ALU.mult))
                elif s[0] == "idx":
                    t, h = s[1], s[2]
                    m = mb[:, MBOFF[t]:MBOFF[t] + NKEY[t]]
                    r = ee[:, 0, ix % 2, 0:NKEY[t]]
                    v.wait_ge(ix_relu, ix + 1)
                    if h == 0:
                        v.tensor_scalar(m, r, wis[:, t, 0:1], None, ALU.mult).then_inc(ix_acc, 1)
                    else:
                        v.wait_ge(ix_acc, ix)
                        v.scalar_tensor_tensor(out=m, in0=r, scalar=wis[:, t, h:h + 1], in1=m, op0=ALU.mult,
                                               op1=ALU.add).then_inc(ix_acc, 1)
                    ix += 1
                elif s[0] == "idxmask":
                    t = s[1]
                    v.wait_ge(ix_acc, ix)
                    if t:
                        link(v.memset(mb[0:64, MBOFF[t] + NKEY[t] - 64:MBOFF[t] + NKEY[t]], OUT_OF_REACH))
                elif s[0] == "topk":
                    t, r = s[1], s[2]
                    m = mb[:, MBOFF[t]:MBOFF[t] + NKEY[t]]
                    link(v.max(top8[:, :], m))
                    link(v.match_replace(out=m, in_to_replace=top8[:, :], in_values=m, imm_value=TAKEN))
                    if r == ROUNDS[t] - 1:
                        link(v.tensor_scalar(m, m, (OUT_OF_REACH + TAKEN) / 2, NEG, ALU.is_gt, ALU.mult))
                elif s[0] == "qk":
                    u = s[1]
                    g, t, diff = unit(u)
                    n = NKEY[t]
                    v.wait_ge(qk_ready, u + 1)
                    if diff:
                        if t:
                            link(v.memset(lg[0:64, :, n - 64:n], NEG))
                        link(v.tensor_reduce(mx[:, u, :], lg[:, :, 0:n], AX.X, ALU.max))
                    else:
                        v.wait_ge(tr_ready, sets_before(u - 1))
                        m_ = mb[:, MBOFF[t]:MBOFF[t] + n]
                        for m in range(2):
                            ins = v.tensor_tensor_reduce(out=ee[:, u % 2, m, 0:n], in0=lg[:, m, 0:n], in1=m_, scale=1.0,
                                                         scalar=NEG, op0=ALU.add, op1=ALU.max,
                                                         accum_out=mx[:, u, m:m + 1])
                            link(ins)
                    v.tensor_scalar(nmx[:, u, :], mx[:, u, :], -SCALE, None, ALU.mult).then_inc(mx_ready, 1)
                elif s[0] == "comb":
                    u = s[1]
                    g, t, diff = unit(u)
                    n = NKEY[t]
                    v.wait_ge(e_ready, u + 1)
                    link(v.reciprocal(rsum[:, u, :], esum[:, u, :]))
                    e0, e1_ = ee[:, u % 2, 0, 0:n], ee[:, u % 2, 1, 0:n]
                    if diff:
                        link(v.tensor_scalar(nlr[:, u:u + 1], rsum[:, u, 1:2], lam[:, 2:3], None, ALU.mult))
                        link(v.tensor_scalar(e1_, e1_, nlr[:, u:u + 1], None, ALU.mult))
                        ins = v.scalar_tensor_tensor(out=e0, in0=e0, scalar=rsum[:, u, 0:1], in1=e1_, op0=ALU.mult,
                                                     op1=ALU.add)
                        if t == 0:
                            link(ins)
                    if t == 0:
                        for m in range(1 if diff else 2):
                            ins = v.memset(ee[:, u % 2, m, n:NBLK[0] * P], 0.0)
                    if diff or t == 0:
                        ins.then_inc(p_ready, 1)
                elif s[0] == "pv":
                    u = s[1]
                    g, t, diff = unit(u)
                    v.wait_ge(pt_used, sets_before(u + 1))
                    if diff:
                        if u == 0:
                            v.wait_ge(ix_full, 32)
                        link(v.tensor_copy(ob[:, u, :], pvb[:, 0:P]))
                        v.tensor_tensor_reduce(out=on[:, :], in0=ob[:, u, :], in1=ob[:, u, :], scale=1.0, scalar=0.0,
                                               op0=ALU.mult, op1=ALU.add, accum_out=osq[:, u:u + 1]).then_inc(o_ready, 1)
                        v.wait_ge(o_ready, u + 1)
                    else:
                        if u == 20:
                            v.wait_ge(pj_full, tile_of[("otr", 7)] + 1)
                        for m in range(2):
                            ins = v.tensor_scalar(ob[:, u - 20, m * HD:m * HD + HD], pvb[:, m * P + m * HD:m * P + m * HD + HD],
                                                  rsum[:, u, m:m + 1], None, ALU.mult)
                        ins.then_inc(o_ready, 1)
                elif s[0] == "bscale":
                    v.wait_ge(on_rms, 1)
                    link(v.reciprocal(orms[:, :], orms[:, :]))
                    link(v.tensor_scalar(orms[:, :], orms[:, :], 1.0 - LAM_INIT, None, ALU.mult))
                    for h in range(4):
                        for t in range(5):
                            n = 5 * h + t
                            ins = v.tensor_scalar(ob[:, n, :], ob[:, n, :], orms[:, n:n + 1], None, ALU.mult)
                        ins.then_inc(on_ready, 1)
            for kc in range(KC):
                v.wait_ge(ot_hi, kc + 1)
                v.tensor_tensor(otl[:, kc, :], oT[:, kc, :], oth[:, kc, :].bitcast(F32), ALU.subtract).then_inc(ot_lo, 1)
            for d in range(KC):
                n = tile_of[("oa", d)]
                v.wait_ge(pj_full, n + 1)
                v.wait_ge(pj_act, taken(tile_of[AT[("gb", d)]], "A"))
                ga, gb = gates[d % 2][:, 0, :], gates[d % 2][:, 1, :]
                v.tensor_tensor(two(ga), pj_view(n), two(ga), ALU.mult).then_inc(pj_dve, 1)
                v.wait_ge(pj_full, n + 2)
                v.tensor_tensor(two(gb), pj_view(n + 1), two(gb), ALU.mult).then_inc(pj_dve, 1)
                v.wait_ge(pj_dve, taken(n + 1, "D"))
                if d:
                    v.wait_ge(m_hi, d)
                    v.wait_ge(m_lo, d)
                v.tensor_tensor(mt[:, :], ga, gb, ALU.add).then_inc(m_ready, 1)
            v.wait_ge(ada_done, 12)
            gain_scale(1, 4 * KC)
            for n, gt in ((0, 2), (1, 5)):
                for w in range(2):
                    link(v.tensor_tensor(gg[:, n, :, w], ada[:, gt * KC:gt * KC + KC, w], gains[:, 2 * n + 1, :], ALU.mult))

            def gated(n, rstd, kc):
                for w, c0, c1 in SPANS:
                    ins = v.scalar_tensor_tensor(out=ymix[:, kc, c0:c1], in0=ymix[:, kc, c0:c1],
                                                 scalar=gg[:, n, kc, w:w + 1], in1=rstd[:, c0:c1], op0=ALU.mult,
                                                 op1=ALU.mult)
                ins.then_inc(yg_ready, 1)

            v.wait_ge(pj_act, taken(tile_of["stat1"], "A"))
            v.reciprocal(rstd1[:, :], rms1[:, :]).then_inc(rstd_ready, 1)
            v.wait_ge(rstd_ready, 2)
            v.wait_ge(xres_in, 16)
            for kc in range(KC):
                gated(0, rstd1, kc)
                if kc % 2:
                    v.wait_ge(yg_ready, kc + 1)
                    v.tensor_tensor(x1[:, kc, :], ymix[:, kc, :], xres[:, kc, :], ALU.add).then_inc(x1_dve, 1)
            v.wait_ge(pj_act, taken(tile_of["stat2"], "A"))
            v.reciprocal(rstd2[:, :], rms1[:, :]).then_inc(rstd_ready, 1)
            v.wait_ge(x1_dve, KC // 2)
            v.wait_ge(x1_pool, KC // 2)
            modulate(1, 3 * KC, lambda kc: xr1[:, kc % 2, :], hf1, hh2, hl2)

            def ffn(i, t0, n_tiles):
                for t in range(t0, t0 + n_tiles):
                    n = T_GU + 2 * t
                    v.wait_ge(pj_full, i * 6 + (n + 2))
                    v.wait_ge(pj_act, i * 3 + taken(n, "A"))
                    if t:
                        v.wait_ge(f_lo, i * 3 + t)
                    v.tensor_tensor(two(ft[:, :]), pj_view(n + 1), two(sg[:, :]), ALU.mult).then_inc(pj_dve, 1)
                    v.wait_ge(pj_dve, i * 3 + taken(n + 1, "D"))
                    v.wait_ge(f_hi, i * 3 + (t + 1))
                    at_ = bass.ds(i * 3 + t, 1)
                    v.tensor_tensor(fl[:, at_, :].rearrange("p a n -> p (a n)"), ft[:, :],
                                    fh[:, at_, :].rearrange("p a n -> p (a n)").bitcast(F32), ALU.subtract).then_inc(f_lo, 1)

            ffn(0, 0, 1)
            with v.Fori(0, FC // 3) as i:
                ffn(i, 1, 3)
            v.wait_ge(pj_act, taken(tile_of["stat3"], "A"))
            v.reciprocal(rstd3[:, :], sq2[:, :]).then_inc(rstd_ready, 1)
            v.wait_ge(rstd_ready, 4)
            for kc in range(KC):
                gated(1, rstd3, kc)
                v.wait_ge(yg_ready, KC + kc + 1)
                v.tensor_tensor(x1[:, kc, :], ymix[:, kc, :], x1[:, kc, :], ALU.add).then_inc(y_fin, 1)

        @block.tensor
        def _(pe):
            mm = pe.matmul
            pe.wait_ge(consts, 2)
            pe.wait_ge(c_lo, 1)

            def ada_chunk(c):
                _, n, q = CH[c]
                tile = tile_of[("ada", n)]
                wait_lo(pe, c)
                if q == 0:
                    pj_free(pe, tile)
                for k in range(2):
                    kc = 2 * q + k
                    for w, part in ((whi, 0), (wlo, 1)):
                        ins = mm(pj[tile % 2][:, 0, :], cstat[:, 4 * kc:4 * kc + P], w[:, slot(c), k * 512:(k + 1) * 512],
                                 start=(kc == 0 and part == 0), stop=(kc == KC - 1 and part == 1))
                ins.then_inc(ada_used, 1)

            def ada_rows(n):
                tile = tile_of[("ada", n)]
                pe.wait_ge(ada_sb, n + 1)
                for k in range(4):
                    ins = pe.transpose(pj[tile % 2][:, 1, 4 * k:4 * k + 4], row[0:4, k * P:(k + 1) * P], ident[0:4, 0:4])
                ins.then_inc(pj_full, 1)

            def stat(tile, src, first, n=KC):
                pj_free(pe, tile)
                for kc in range(n):
                    pe.wait_ge(sq_ready, first + kc + 1)
                    for h in range(2):
                        x = src(kc)[:, h * HALF:(h + 1) * HALF]
                        ins = mm(pj[tile % 2][:, h, 0:HALF], ones[:, :], x, start=(kc == 0), stop=(kc == n - 1))
                    ins.then_inc(sq_used if kc < n - 1 else pj_full, 1)

            def blocks(c, tile, kcs, xh, xl, first, last):
                for kc in kcs:
                    b = kc * P
                    for w, x in ((whi, xh), (whi, xl), (wlo, xh)):
                        for h in range(2):
                            ins = mm(pj[tile % 2][:, h, 0:HALF], w[:, slot(c), b:b + P], x[:, kc, h * HALF:(h + 1) * HALF],
                                     start=(kc == first and w is whi and x is xh),
                                     stop=(kc == last and w is wlo))
                return ins

            for c in range(N_ADA0):
                ada_chunk(c)
                if c == 3:
                    pe.wait_ge(misc_in, 16 * 5)
                if c % 4 == 3:
                    ada_rows(c // 4)
                if c == RAW0 - 1:
                    stat(tile_of["stat0"], lambda kc: sq0[:, kc % 2, :], 0)

            ix = 0
            sets = 0
            pe.wait_ge(h_lo, 1)
            for s in SCHED:
                if s[0] == "part":
                    c, k0, k1 = s[1], s[2], s[3]
                    if k0 == 0:
                        wait_lo(pe, c)
                        pj_free(pe, tile_of[c])
                    for kc in range(k0, k1):
                        if c == N_ADA0:
                            pe.wait_ge(h_lo, kc + 1)
                        ins = blocks(c, tile_of[c], [kc], hh, hl, 0, KC - 1)
                        if kc == KC - 1:
                            ins.then_inc(pj_full, 1)
                elif s[0] == "ada":
                    ada_chunk(s[1])
                elif s[0] == "adarow":
                    ada_rows(s[1])
                elif s[0] == "otr":
                    src, dst = s[1], s[2]
                    tile = tile_of[("otr", dst)]
                    pj_free(pe, tile)
                    if dst >= 4:
                        pe.wait_ge(on_ready, src + 1)
                    else:
                        pe.wait_ge(o_ready, 20 + 5 * (src + 1))
                    for t in range(5):
                        to = pj[tile % 2][:, 0, P * (t - 1):P * t] if t else pj[tile % 2][:, 1, 0:P]
                        ins = pe.transpose(to, ob[:, 5 * src + t, :], ident[:, :])
                    ins.then_inc(pj_full, 1)
                elif s[0] == "vload":
                    wait_lo(pe, AT[("v", KC - 1)])
                elif s[0] == "v":
                    t = s[1]
                    tile = tile_of[("v", t)]
                    pj_free(pe, tile)
                    q = slice(QCOL[t], QCOL[t] + P)
                    for kc in range(KC):
                        for x, w in ((hh, wv_h), (hh, wv_l), (hl, wv_h)):
                            for h in range(2):
                                ins = mm(pj[tile % 2][:, h, 0:VH], x[:, kc, q], w[:, kc, h * VH:(h + 1) * VH],
                                         start=(kc == 0 and w is wv_h and x is hh), stop=(kc == KC - 1 and x is hl))
                    ins.then_inc(pj_full, 1)
                elif s[0] == "idx":
                    t, h = s[1], s[2]
                    if ix == 0:
                        pe.wait_ge(rope_lo, N_KI)
                    if ix >= 2:
                        pe.wait_ge(ix_relu, ix - 1)
                    j, m = divmod(h, 2)
                    logits(pe, lg[:, ix % 2, 0:NMOV[t]], qi_h[:, j, :], qi_l[:, j, :], ki, m, t).then_inc(ix_full, 1)
                    ix += 1
                elif s[0] == "qk":
                    u = s[1]
                    g, t, diff = unit(u)
                    if u == 0:
                        pe.wait_ge(ix_relu, 32)
                    elif unit(u - 1)[2]:
                        pe.wait_ge(e_ready, u)
                    else:
                        pe.wait_ge(mx_ready, u)
                    pe.wait_ge(rope_lo, last_rope(g) + 1)
                    qt = q1 if g % 2 else q0
                    kt = (kz1 if g % 2 else kz0) if diff else kz0
                    for m in range(2):
                        ins = logits(pe, lg[:, m, 0:NMOV[t]], qt[:, 0, :], qt[:, 1, :], kt, m, t)
                    ins.then_inc(qk_ready, 1)
                elif s[0] == "tr" and not (s[2] and s[1] < 20):
                    u, m = s[1], s[2]
                    g, t, diff = unit(u)
                    if diff or t == 0:
                        pe.wait_ge(p_ready, u + 1 if diff else 21 + (u - 20) // 5)
                    else:
                        pe.wait_ge(e_ready, u + 1)
                    if sets:
                        pe.wait_ge(pt_ready, sets)
                    for b in range(NBLK[t]):
                        ins = pe.transpose(tb[:, b * P:(b + 1) * P], ee[:, u % 2, m, b * P:(b + 1) * P], ident[:, :])
                    ins.then_inc(tr_ready, 1)
                    sets += 1
                elif s[0] == "pv":
                    u = s[1]
                    g, t, diff = unit(u)
                    if u:
                        pe.wait_ge(o_ready, u)
                    if u == 0:
                        pe.wait_ge(vcache_in, 16)
                    for m in range(1 if diff else 2):
                        n = sets_before(u) + m
                        pe.wait_ge(pt_ready, n + 1)
                        col = AKV + P * g if diff else 0
                        at_ = m * P
                        for b in range(NBLK[t]):
                            ins = mm(pvb[:, at_:at_ + P], pt[:, n % 3, b * P:(b + 1) * P],
                                     vt[:, VBLK[t] + b, col:col + P], start=(b == 0), stop=(b == NBLK[t] - 1))
                        ins.then_inc(pt_used, 1)
            for d in range(KC):
                if d + 1 < KC:
                    for name in ("ga", "gb"):
                        c = AT[(name, d + 1)]
                        wait_lo(pe, c)
                        pj_free(pe, tile_of[c])
                        blocks(c, tile_of[c], range(KC), hh, hl, 0, KC - 1).then_inc(pj_full, 1)
                c = AT[("wo", d)]
                wait_lo(pe, c)
                for i, name in enumerate(("oa", "ob")):
                    tile = tile_of[(name, d)]
                    pj_free(pe, tile)
                    if d == 0:
                        pe.wait_ge(ot_lo, 4 * i + 4)
                    blocks(c, tile, range(4 * i, 4 * i + 4), oth, otl, 4 * i, 4 * i + 3).then_inc(pj_full, 1)
            for d in range(KC):
                tile = T_OUT + d
                wait_lo(pe, C_OUT + d)
                pj_free(pe, tile)
                for kc in range(KC):
                    if d == 0:
                        pe.wait_ge(m_lo, kc + 1)
                    ins = blocks(C_OUT + d, tile, [kc], mh, ml, 0, KC - 1)
                ins.then_inc(pj_full, 1)
            pe.wait_ge(acc_ready, KC)
            tile = tile_of["stat1"]
            pj_free(pe, tile)
            for h in range(2):
                ins = mm(pj[tile % 2][:, h, 0:HALF], ones[:, :], acc1[:, h * HALF:(h + 1) * HALF], start=True, stop=True)
            ins.then_inc(pj_full, 1)
            stat(tile_of["stat2"], lambda kc: sq1[:, kc % 2, :], KC)

            def gu(i, t0, n_tiles):
                for q in range(2 * t0, 2 * (t0 + n_tiles)):
                    tile = T_GU + q
                    pe.wait_ge(w_lo, i * 6 + lo_count(C_GU + q))
                    if q >= 2:
                        who = takers[tile - 2]
                        pe.wait_ge(pj_act if who == "A" else pj_dve, i * 3 + taken(tile - 2, who))
                    else:
                        pj_free(pe, tile)
                    for kc in range(KC):
                        if q == 0:
                            pe.wait_ge(h_lo, KC + kc + 1)
                        ins = blocks(C_GU + q, tile, [kc], hh2, hl2, 0, KC - 1)
                    ins.then_inc(pj_full, 1)

            gu(0, 0, 1)
            with pe.Fori(0, FC // 3) as i:
                gu(i, 1, 3)
            for d in range(KC):
                tile = T_DN + d
                pj_free(pe, tile)
                for k in range(2):
                    cc = C_DN + 2 * d + k
                    pe.wait_ge(w_lo, lo_count(cc))
                    if d == 0 and k == 0:
                        pe.wait_ge(f_lo, BLK_DOWN)
                    for b in range(BLK_DOWN):
                        kc = BLK_DOWN * k + b
                        if d == 0 and k:
                            pe.wait_ge(f_lo, kc + 1)
                        for w, x in ((dhi, fh), (dhi, fl), (dlo, fh)):
                            for h in range(2):
                                ins = mm(pj[tile % 2][:, h, 0:HALF], w[k][:, b * P:(b + 1) * P],
                                         x[:, kc, h * HALF:(h + 1) * HALF],
                                         start=(kc == 0 and w is dhi and x is fh), stop=(kc == FC - 1 and w is dlo))
                    ins.then_inc(pj_full if k else down_used, 1)
            pe.wait_ge(acc_ready, 2 * KC)
            tile = tile_of["stat3"]
            pj_free(pe, tile)
            for h in range(2):
                ins = mm(pj[tile % 2][:, h, 0:HALF], ones[:, :], acc2[:, h * HALF:(h + 1) * HALF], start=True, stop=True)
            ins.then_inc(pj_full, 1)


def logits(pe, dst, qh, ql, kt, m, t):
    n = NMOV[t]
    q, k = slice(QCOL[t], QCOL[t] + P), slice(KCOL[t], KCOL[t] + n)
    pe.matmul(dst, qh[:, q], kt[:, 0, m, k], start=True, stop=False)
    pe.matmul(dst, ql[:, q], kt[:, 0, m, k], start=False, stop=False)
    return pe.matmul(dst, qh[:, q], kt[:, 1, m, k], start=False, stop=True)


def pair(a, b):
    h = HD // 2
    return [*range(a, a + h), *range(b, b + h), *range(a + h, a + HD), *range(b + h, b + HD)]


C_QA, C_KA, C_VA, C_QI = 0, AW, AW + AKV, AW + 2 * AKV
C_KI = C_QI + IQ
C_WI = C_KI + HD
C_QB = C_WI + IH
C_KB, C_VB = C_QB + BW, C_QB + 2 * BW
C_GA = C_VB + BW
C_GB = C_GA + D

IN_CHUNKS = ([(("ki", 0), pair(C_KI, C_KI))]
             + [(("qi", j), pair(C_QI + 2 * j * HD, C_QI + (2 * j + 1) * HD)) for j in range(4)]
             + [((n, h), pair(b + P * h, b + P * h + HD)) for h in range(4) for n, b in (("kb", C_KB), ("qb", C_QB))]
             + [(("ka", 0), pair(C_KA, C_KA + HD))]
             + [(("qa", j), pair(C_QA + j * HD, C_QA + (j + 4) * HD)) for j in range(4)]
             + [((n, d), list(range(b + P * d, b + P * (d + 1)))) for d in range(KC) for n, b in (("ga", C_GA), ("gb", C_GB))])
W_ROW = {name: i for i, (name, _) in enumerate(IN_CHUNKS)}
S_WO = len(IN_CHUNKS)
W_ROW.update({("wo", d): S_WO + d for d in range(KC)})
S_OUT = S_WO + KC


def kernel(**inputs):
    import numpy as _np
    import concourse.bacc as _bacc
    from concourse import mybir as _mybir
    from concourse.bass_utils import run_bass_kernel_spmd as _run

    x = {k: _np.asarray(v) for k, v in inputs.items()}

    def chunk(w):
        return w.reshape(-1, P, w.shape[1]).transpose(1, 0, 2).reshape(P, -1)

    def columns(v):
        return v.reshape(-1, P).T

    w_in = x["w_in"][0]
    ws = [chunk(w_in[:, cols]) for _, cols in IN_CHUNKS]
    rows_a = [r for j in range(4) for b in (j, j + 4) for r in range(b * HD, (b + 1) * HD)]
    w_o = _np.concatenate([x["w_o_a"][0][rows_a], x["w_o_b"][0]], axis=0)
    ws += [chunk(w_o[:, d * P:(d + 1) * P]) for d in range(KC)]
    ws += [chunk(x["w_out"][0][:, d * P:(d + 1) * P]) for d in range(KC)]
    for i in range(FC):
        ws += [chunk(x[n][0][:, i * P:(i + 1) * P]) for n in ("w_gate", "w_up")]
    v_cols = [*range(C_VA, C_VA + AKV), *range(C_VB, C_VB + BW), *range(C_WI, C_WI + IH)]
    w_d = _np.stack([chunk(x["w_down"][0][k * BLK_DOWN * P:(k + 1) * BLK_DOWN * P, d * P:(d + 1) * P])
                     for d in range(KC) for k in range(2)])
    w_ada = _np.stack([chunk(x["w_ada"][0][q * 256:(q + 1) * 256, n * 512:(n + 1) * 512])
                       for n in range(12) for q in range(4)])
    tokens = _np.concatenate([x["x_sample"][0], x["x_prompt"][0]], axis=0)
    pos = _np.concatenate([PAST + _np.arange(NS), _np.arange(NP_)]).astype(_np.float32)
    half = HD // 2
    inv = (1.0 / (_np.float32(10000.0) ** (_np.arange(half, dtype=_np.float32) / _np.float32(half)))).astype(_np.float32)
    ang = (pos[None, :] * inv[:, None]).astype(_np.float32)
    cos, sin = _np.cos(ang).astype(_np.float32), _np.sin(ang).astype(_np.float32)
    own = (_np.arange(P) // half) % 2
    ck = {"ki": [x["cache_idx_k"][0, 0]] * 2, "ka": [x["cache_a_k"][0, 0, :, j] for j in range(2)]}
    caches = []
    for name, j in KTILES:
        a_, b_ = ck[name] if name in ck else [x["cache_b_k"][0, 0, :, j, m] for m in range(2)]
        both = _np.concatenate([a_, b_], axis=1).T
        caches.append(both[pair(0, HD)])
    cv = _np.concatenate([x["cache_a_v"][0, 0].reshape(PAST, AKV), x["cache_b_v"][0, 0].reshape(PAST, BW)], axis=1)
    arrays = {
        "w_s": _np.stack(ws), "w_v": w_in[:, v_cols].reshape(KC, P, VWI), "w_ada": w_ada, "w_d": w_d,
        "xT": tokens.T.reshape(KC, P, T).transpose(1, 0, 2),
        "cT": _np.stack([columns(x["c_prompt"][0]), columns(x["c_sample"][0])], axis=2),
        "bada": _np.stack([columns(x["b_ada"][0])] * 2, axis=2),
        "gains": _np.stack([columns(x[n][0]) for n in ("g_pre_mix", "g_post_mix", "g_pre_ffn", "g_post_ffn")], axis=1),
        "lamv": _np.broadcast_to(_np.stack([x[n][0] for n in ("lam_q1", "lam_q2", "lam_k1", "lam_k2")])[None], (P, 4, HD)),
        "hmask": _np.stack([own == 0, own == 1], axis=1).astype(_np.float32),
        "cos": _np.tile(cos, (4, 1)), "sin": _np.concatenate([sin, sin, -sin, -sin], axis=0),
        "ident": _np.eye(P, dtype=_np.float32),
        "cache_k": _np.stack(caches), "cache_v": cv.reshape(2, P, VW).transpose(1, 0, 2),
    }
    arrays = {k: _np.ascontiguousarray(v) for k, v in arrays.items()}
    nc = _bacc.Bacc("TRN2", target_bir_lowering=False, num_devices=1)
    a = {k: nc.dram_tensor("in_" + k, v.shape, _mybir.dt.from_np(v.dtype), kind="ExternalInput").ap()
         for k, v in arrays.items()}
    outs = {"yT": (KC, P, T), "kT": (len(KTILES), P, T), "v_p": (P, 4, VW), "v_s": (NS, VW)}
    o = {k: nc.dram_tensor("out_" + k, s, F32, kind="ExternalOutput").ap() for k, s in outs.items()}
    build(nc, a, o)
    r = _run(nc, [{"in_" + k: v for k, v in arrays.items()}], core_ids=[0]).results[0]

    y = r["out_yT"].reshape(D, T).T
    back = _np.argsort(pair(0, HD))
    k = r["out_kT"][:, back].transpose(0, 2, 1)
    vp = r["out_v_p"].transpose(1, 0, 2).reshape(NP_, VW)
    vs = r["out_v_s"]
    kb = _np.stack([k[KT_AT[("kb", h)]] for h in range(4)], axis=1)
    res = [y[NS:].reshape(1, NP_, D), y[:NS].reshape(1, NS, D)]
    for rows, v in ((slice(NS, T), vp), (slice(0, NS), vs)):
        n = v.shape[0]
        res += [k[KT_AT[("ka", 0)]][rows].reshape(1, 1, n, 2, HD), v[:, :AKV].reshape(1, 1, n, 2, HD),
                k[0][rows][:, :HD].reshape(1, 1, n, HD), kb[rows].reshape(1, 1, n, 4, 2, HD),
                v[:, AKV:].reshape(1, 1, n, 4, 2 * HD)]
    return tuple(_np.ascontiguousarray(t) for t in res)
```
